# Optimizing a Trainium2 kernel written in Bass

```python
import jax
import jax.numpy as jnp
from jax import lax
import numpy as np

D_MODEL = 1024
BATCH = 1
SEQ = 256
DEPTH = 2

D_MIX = D_MODEL
MLSTM_HEADS = 4
MLSTM_DQK = D_MODEL // 8
MLSTM_DV = D_MODEL // 8
MLSTM_WIDTH = MLSTM_HEADS * MLSTM_DV
CONV_WIDTH = D_MIX - MLSTM_WIDTH
CONV_K = 3
CHUNK = 64
N_GROUPS = 4
EXPERTS_PER_GROUP = 4
TOP_K = 2
D_EXPERT = D_MODEL // 2
ALPHA = (2 * DEPTH) ** 0.25
BETA = (8 * DEPTH) ** -0.25
LN_EPS = 1e-5
IN_SIZES = (MLSTM_HEADS * MLSTM_DQK, MLSTM_HEADS * MLSTM_DQK, MLSTM_WIDTH, MLSTM_WIDTH,
            MLSTM_HEADS, MLSTM_HEADS, CONV_WIDTH, CONV_WIDTH, CONV_WIDTH)
D_IN = sum(IN_SIZES)

kernel_name = 'hybrid_mlstm_shortconv_hiermoe_deepnorm_adaln'

def layer_norm(x, g, b):
    xf = x.astype(jnp.float32)
    mu = xf.mean(-1, keepdims=True)
    var = jnp.square(xf - mu).mean(-1, keepdims=True)
    y = (xf - mu) * lax.rsqrt(var + LN_EPS) * g.astype(jnp.float32) + b.astype(jnp.float32)
    return y.astype(x.dtype)

def head_norm(h, w):
    bsz, seq, nh, dv = h.shape
    mu = h.mean(-1, keepdims=True)
    var = jnp.square(h - mu).mean(-1, keepdims=True)
    hn = (h - mu) * lax.rsqrt(var + LN_EPS)
    return hn.reshape(bsz, seq, nh * dv) * w.astype(jnp.float32)

def mlstm_chunkwise(q, k, v, i_pre, f_pre):
    f32 = jnp.float32
    bsz, seq, nh, dk = q.shape
    dv = v.shape[-1]
    nc = seq // CHUNK

    def to_chunks(t):
        t = t.astype(f32).reshape((bsz, nc, CHUNK, nh) + t.shape[3:])
        return jnp.moveaxis(t, 3, 1)

    qc = to_chunks(q) * (dk ** -0.5)
    kc = to_chunks(k)
    vc = to_chunks(v)
    ig = to_chunks(i_pre)
    logf = jax.nn.log_sigmoid(to_chunks(f_pre))
    bcum = jnp.cumsum(logf, axis=-1)
    gtot = bcum[..., -1]

    causal = jnp.tril(jnp.ones((CHUNK, CHUNK), dtype=bool))
    dmat = jnp.where(causal, bcum[..., :, None] - bcum[..., None, :] + ig[..., None, :], -jnp.inf)

    a = gtot[..., None] - bcum + ig
    m_loc = a.max(-1)
    w_loc = jnp.exp(a - m_loc[..., None])
    c_loc = jnp.einsum('bhcsv,bhcsk->bhcvk', w_loc[..., None] * vc, kc)
    n_loc = jnp.einsum('bhcs,bhcsk->bhck', w_loc, kc)

    def step(carry, xs):
        c_st, n_st, m_st = carry
        g_c, m_c, cl, nl = xs
        m_new = jnp.maximum(g_c + m_st, m_c)
        decay = jnp.exp(g_c + m_st - m_new)
        inj = jnp.exp(m_c - m_new)
        c_new = decay[..., None, None] * c_st + inj[..., None, None] * cl
        n_new = decay[..., None] * n_st + inj[..., None] * nl
        return (c_new, n_new, m_new), (c_st, n_st, m_st)

    init = (jnp.zeros((bsz, nh, dv, dk), f32), jnp.zeros((bsz, nh, dk), f32),
            jnp.zeros((bsz, nh), f32))
    xs = (jnp.moveaxis(gtot, 2, 0), jnp.moveaxis(m_loc, 2, 0),
          jnp.moveaxis(c_loc, 2, 0), jnp.moveaxis(n_loc, 2, 0))
    _, (c_prev, n_prev, m_prev) = lax.scan(step, init, xs)
    c_prev = jnp.moveaxis(c_prev, 0, 2)
    n_prev = jnp.moveaxis(n_prev, 0, 2)
    m_prev = jnp.moveaxis(m_prev, 0, 2)

    e_inter = bcum + m_prev[..., None]
    m_t = jnp.maximum(e_inter, dmat.max(-1))
    s_mat = jnp.einsum('bhctk,bhcsk->bhcts', qc, kc) * jnp.exp(dmat - m_t[..., None])
    w_inter = jnp.exp(e_inter - m_t)
    num = (jnp.einsum('bhcts,bhcsv->bhctv', s_mat, vc)
           + w_inter[..., None] * jnp.einsum('bhcvk,bhctk->bhctv', c_prev, qc))
    den = s_mat.sum(-1) + w_inter * jnp.einsum('bhck,bhctk->bhct', n_prev, qc)
    h = num / jnp.maximum(jnp.abs(den), jnp.exp(-m_t))[..., None]
    return jnp.moveaxis(h, 1, 3).reshape(bsz, seq, nh, dv)

def short_gated_conv(b_gate, c_gate, h_in, w_conv):
    z = c_gate * h_in
    zc = lax.conv_general_dilated(z, w_conv[:, None, :], window_strides=(1,),
                                  padding=[(CONV_K - 1, 0)],
                                  dimension_numbers=('NWC', 'WIO', 'NWC'),
                                  feature_group_count=z.shape[-1])
    return b_gate * zc

def hier_moe(u, w_grp, b_grp, w_router, b_router, w_gate, w_up, w_down):
    f32 = jnp.float32
    bsz, seq, dm = u.shape
    t = u.reshape(bsz * seq, dm)
    grp_logits = (t @ w_grp + b_grp).astype(f32)
    grp_prob = jax.nn.softmax(grp_logits, axis=-1)
    grp_idx = jnp.argmax(grp_logits, axis=-1)
    grp_w = jnp.take_along_axis(grp_prob, grp_idx[:, None], axis=-1)
    exp_logits = (t @ w_router + b_router).astype(f32).reshape(-1, N_GROUPS, EXPERTS_PER_GROUP)
    sel_logits = jnp.take_along_axis(exp_logits, grp_idx[:, None, None], axis=1)[:, 0]
    top_vals, top_idx = lax.top_k(sel_logits, TOP_K)
    top_w = jax.nn.softmax(top_vals, axis=-1) * grp_w
    exp_w = jnp.einsum('tk,tke->te', top_w, jax.nn.one_hot(top_idx, EXPERTS_PER_GROUP, dtype=f32))
    comb = (jax.nn.one_hot(grp_idx, N_GROUPS, dtype=f32)[:, :, None] * exp_w[:, None, :]).astype(u.dtype)
    y = jnp.zeros_like(t)
    for gi in range(N_GROUPS):
        hg = (jax.nn.silu(jnp.einsum('td,edf->tef', t, w_gate[gi]))
              * jnp.einsum('td,edf->tef', t, w_up[gi]))
        y = y + jnp.einsum('tef,efd->td', hg * comb[:, gi, :, None], w_down[gi])
    return y.reshape(bsz, seq, dm)

def setup_inputs(seed: int = 0) -> dict:
    key = jax.random.key(seed)
    ks = jax.random.split(key, 24)
    nrm = jax.random.normal
    H = MLSTM_HEADS
    G, E, F = N_GROUPS, EXPERTS_PER_GROUP, D_EXPERT
    x = nrm(ks[0], (BATCH, SEQ, D_MODEL), jnp.float32)
    c = nrm(ks[1], (BATCH, D_MODEL), jnp.float32)
    w_ada = nrm(ks[2], (DEPTH, D_MODEL, 6 * D_MODEL)) * (0.2 * D_MODEL ** -0.5)
    b_ada = 0.02 * nrm(ks[3], (DEPTH, 6 * D_MODEL))
    w_in = nrm(ks[4], (DEPTH, D_MODEL, D_IN)) * D_MODEL ** -0.5
    b_i = 0.1 * nrm(ks[5], (DEPTH, H))
    b_f = jnp.linspace(3.0, 6.0, H)[None, :] + 0.1 * nrm(ks[6], (DEPTH, H))
    b_gates = jnp.concatenate([b_i, b_f], axis=-1)
    mh_norm_w = 1.0 + 0.02 * nrm(ks[7], (DEPTH, MLSTM_WIDTH))
    w_conv = nrm(ks[8], (DEPTH, CONV_K, CONV_WIDTH)) * CONV_K ** -0.5
    w_out = nrm(ks[9], (DEPTH, D_MIX, D_MODEL)) * (BETA * D_MIX ** -0.5)
    ln1_g = 1.0 + 0.02 * nrm(ks[10], (DEPTH, D_MODEL))
    ln1_b = 0.02 * nrm(ks[11], (DEPTH, D_MODEL))
    w_grp = nrm(ks[12], (DEPTH, D_MODEL, G)) * D_MODEL ** -0.5
    b_grp = 0.01 * nrm(ks[13], (DEPTH, G))
    w_router = nrm(ks[14], (DEPTH, D_MODEL, G * E)) * D_MODEL ** -0.5
    b_router = 0.01 * nrm(ks[15], (DEPTH, G * E))
    w_gate = nrm(ks[16], (DEPTH, G, E, D_MODEL, F)) * D_MODEL ** -0.5
    w_up = nrm(ks[17], (DEPTH, G, E, D_MODEL, F)) * D_MODEL ** -0.5
    w_down = nrm(ks[18], (DEPTH, G, E, F, D_MODEL)) * (BETA * F ** -0.5)
    ln2_g = 1.0 + 0.02 * nrm(ks[19], (DEPTH, D_MODEL))
    ln2_b = 0.02 * nrm(ks[20], (DEPTH, D_MODEL))
    return {'x': x, 'c': c, 'w_ada': w_ada, 'b_ada': b_ada, 'w_in': w_in, 'b_gates': b_gates,
            'mh_norm_w': mh_norm_w, 'w_conv': w_conv, 'w_out': w_out, 'ln1_g': ln1_g,
            'ln1_b': ln1_b, 'w_grp': w_grp, 'b_grp': b_grp, 'w_router': w_router,
            'b_router': b_router, 'w_gate': w_gate, 'w_up': w_up, 'w_down': w_down,
            'ln2_g': ln2_g, 'ln2_b': ln2_b}

def reference(x, c, w_ada, b_ada, w_in, b_gates, mh_norm_w, w_conv, w_out, ln1_g, ln1_b,
              w_grp, b_grp, w_router, b_router, w_gate, w_up, w_down, ln2_g, ln2_b):
    bsz, seq, _ = x.shape
    H = MLSTM_HEADS
    split_at = np.cumsum(IN_SIZES)[:-1].tolist()
    cond = jax.nn.silu(c)
    for l in range(DEPTH):
        mod = cond @ w_ada[l] + b_ada[l]
        sh1, sc1, gt1, sh2, sc2, gt2 = [m[:, None, :] for m in jnp.split(mod, 6, axis=-1)]
        u = x * (1 + sc1) + sh1
        proj = u @ w_in[l]
        q, k, v, o, i_pre, f_pre, cb, cc, ch = jnp.split(proj, split_at, axis=-1)
        i_pre = i_pre + b_gates[l, :H]
        f_pre = f_pre + b_gates[l, H:]
        h = mlstm_chunkwise(q.reshape(bsz, seq, H, MLSTM_DQK), k.reshape(bsz, seq, H, MLSTM_DQK),
                            v.reshape(bsz, seq, H, MLSTM_DV), i_pre, f_pre)
        h = head_norm(h, mh_norm_w[l]) * jax.nn.sigmoid(o.astype(jnp.float32))
        y_conv = short_gated_conv(cb, cc, ch, w_conv[l])
        mix = jnp.concatenate([h.astype(x.dtype), y_conv], axis=-1) @ w_out[l]
        x = layer_norm(ALPHA * x + (1 + gt1) * mix, ln1_g[l], ln1_b[l])
        u = x * (1 + sc2) + sh2
        y = hier_moe(u, w_grp[l], b_grp[l], w_router[l], b_router[l], w_gate[l], w_up[l], w_down[l])
        x = layer_norm(ALPHA * x + (1 + gt2) * y, ln2_g[l], ln2_b[l])
    return x


_drawn_inputs = setup_inputs


def setup_inputs(seed=0):
    import zlib

    import numpy as np

    out = dict(_drawn_inputs(seed))
    spreads = {}
    factors = {'mh_norm_w': 8.0, 'b_grp': 23.018, 'b_router': 20.486}
    for name, (base, spread) in spreads.items():
        noise = np.random.default_rng([zlib.crc32(name.encode()), seed]).standard_normal(out[name].shape)
        drawn = base * np.exp(spread * noise) if base else spread * noise
        out[name] = jnp.asarray(drawn.astype(out[name].dtype))
    for name, factor in factors.items():
        out[name] = (out[name] * factor).astype(out[name].dtype)
    return out
```

```python
from contextlib import ExitStack

import concourse.bass as bass
from concourse import mybir

ACT = mybir.ActivationFunctionType
ALU = mybir.AluOpType
AX = mybir.AxisListType
F32 = mybir.dt.float32
BF16 = mybir.dt.bfloat16
I32 = mybir.dt.int32

P = 128
HEADS = 4
EPS = 1e-5
CAP = 64
MASKED = -1e30


def trunk_kernel(nc, x, c, w_ada, b_ada, w_in, b_gates, mh_norm_w, w_conv, w_out, ln1_g, ln1_b,
                 w_grp, b_grp, w_router, b_router, w_gate, w_up, w_down, ln2_g, ln2_b, out):
    _, SEQ, D = x.shape
    DEPTH = w_in.shape[0]
    G, E, _, F = w_gate.shape[1:]
    T = SEQ // P
    KC = D // P
    FC = F // P
    DK = D // 8
    WM = HEADS * DK
    CH = WM // P
    EXPERTS = G * E
    PAIRS = EXPERTS // 2
    ROUNDS = SEQ // CAP
    NMOD = 6 * D // P
    ALPHA = float((2 * DEPTH) ** 0.25)
    SCALE = float(DK) ** -0.5
    assert T == 2 and DK == P and WM == 512 and 2 * CAP == P and CH == HEADS and F == 512

    RING = 6
    COLS = 512
    ADA1, PROJ, ADA2, WOUT, ADA3, ADA4, MOE = 0, 4, 11, 13, 15, 19, 21
    UNITS = MOE + 6 * PAIRS
    NBLK = 24
    COL_GATES = 4 * WM
    PROJ_COL = [0, WM, 2 * WM, 3 * WM, COL_GATES + 8 + WM, COL_GATES + 8 + 2 * WM, COL_GATES + 8]
    ADA_UNIT = [ADA1 + i for i in range(4)] + [ADA2, ADA2 + 1] + [ADA3 + i for i in range(4)] + [ADA4, ADA4 + 1]

    ctx = ExitStack()
    with ctx:
        def sb(name, shape, dt=F32):
            return ctx.enter_context(nc.sbuf_tensor(name, shape, dt))

        def sem(name):
            return ctx.enter_context(nc.semaphore(name))

        bank = [ctx.enter_context(nc.psum_tensor(f"bank{i}", [P, COLS], F32)) for i in range(8)]

        ring = [sb(f"ring{i}", [P, KC, COLS]) for i in range(RING)]
        w_gates_sb = sb("w_gates_sb", [P, DEPTH, KC, 8])
        w_route_sb = sb("w_route_sb", [P, DEPTH, KC, G + EXPERTS])
        ident = sb("ident", [P, P])
        causal = sb("causal", [P, 3 * P])
        before = sb("before", [P, P])
        ones = sb("ones", [P, P])
        partials = sb("partials", [P, P])
        pick_i = sb("pick_i", [8, HEADS])
        pick_f = sb("pick_f", [8, HEADS])
        pick_negf = sb("pick_negf", [8, HEADS])
        head_row = sb("head_row", [HEADS, HEADS, P])
        slots = sb("slots", [P, CAP])
        prefer = sb("prefer", [P, G])
        zeros = sb("zeros", [P, COLS], BF16)
        b_gates_col = sb("b_gates_col", [8, DEPTH])
        b_route_col = sb("b_route_col", [G + EXPERTS, DEPTH])
        b_ada_col = sb("b_ada_col", [P, DEPTH, NMOD])
        w_conv_col = sb("w_conv_col", [P, DEPTH, 3 * CH])
        cond = sb("cond", [P, KC, 32])
        mh_w = sb("mh_w", [P, WM])
        ln_g = sb("ln_g", [P, 2, D])
        ln_b = sb("ln_b", [P, 2, D])
        gate_row = sb("gate_row", [P, 2, D])
        mod = sb("mod", [P, 4, KC])
        part = sb("part", [P, 2, COLS])
        X = sb("X", [P, T, D])
        uT = sb("uT", [P, KC, SEQ])
        qT = sb("qT", [P, HEADS, SEQ])
        kT = sb("kT", [P, HEADS, SEQ])
        v_ext = sb("v_ext", [P, T, HEADS, DK + 1])
        o_sig = sb("o_sig", [P, T, WM])
        ccT = sb("ccT", [P, CH, SEQ])
        zT = sb("zT", [P, CH, 2 + SEQ])
        convT = sb("convT", [P, SEQ])
        mixT = sb("mixT", [P, KC, SEQ])
        gate_pre, gate_neg, gate_ln = mixT[0:8, 0, :], mixT[0:8, 1, :], mixT[0:8, 2, :]
        a_row, neg_g, neg_m = mixT[0:HEADS, 3, :], mixT[0:HEADS, 4, :], mixT[0:HEADS, 5, :]
        hb = sb("hb", [P, T, WM])
        expo = sb("expo", [P, HEADS, 3 * P])
        b_ada_rows = expo[0:NMOD, 0, 0:DEPTH * P].rearrange("r (l p) -> r l p", l=DEPTH)
        w_conv_rows = expo[0:3 * CH, 1, 0:DEPTH * P].rearrange("r (l p) -> r l p", l=DEPTH)
        c_rows = expo[0:KC, 2, 0:P]
        cums = [sb(f"cums{i}", [8, P + SEQ]) for i in range(2)]
        maxs = [sb(f"maxs{i}", [HEADS, P + SEQ]) for i in range(2)]
        a_col = sb("a_col", [P, T, HEADS])
        exp_neg_m = sb("exp_neg_m", [P, T, HEADS])
        den = sb("den", [P, T, HEADS])
        dmax = sb("dmax", [P, T, HEADS])
        stats_h = sb("stats_h", [P, T * HEADS, 6])
        mv_h = sb("mv_h", [P, T * HEADS, 2])
        stats = sb("stats", [P, T, 2, 6])
        mv = sb("mv", [P, T, 2])
        var = sb("var", [P, 8])
        lnv = sb("lnv", [P, 8])
        rstd = sb("rstd", [P, 8])
        nt = sb("nt", [P, 8])
        tmp = sb("tmp", [P, COLS])
        logT = sb("logT", [G + EXPERTS, SEQ])
        logit = sb("logit", [P, T, G + EXPERTS])
        gmax = sb("gmax", [P, T, 1])
        grp1 = sb("grp1", [P, T, G])
        ew = sb("ew", [P, T, G, E])
        sel = sb("sel", [P, T, E])
        sel2 = sb("sel2", [P, T, E])
        top1 = sb("top1", [P, T, E])
        top2 = sb("top2", [P, T, E])
        m1 = sb("m1", [P, T, 1])
        m2 = sb("m2", [P, T, 1])
        sc = sb("sc", [P, T, E])
        scm = sb("scm", [P, T, 1])
        dif = sb("dif", [P, T, G + 1])
        dexp = sb("dexp", [P, T, G + 1])
        wsum = sb("wsum", [P, T, 3])
        both = sb("both", [P, T, E])
        wboth = sb("wboth", [P, T, E])
        comb = sb("comb", [P, T, EXPERTS])
        mask = sb("mask", [P, T, EXPERTS])
        pos = sb("pos", [P, T, EXPERTS])
        pmax = sb("pmax", [P, 1])
        pall = sb("pall", [1, 1])
        flag = sb("flag", [1, DEPTH], I32)
        disp = [ccT[:, i, :].rearrange("p (t s) -> p t s", t=T) for i in range(2)]
        dispw = [ccT[:, 2 + i, :].rearrange("p (t s) -> p t s", t=T) for i in range(2)]
        xg = qT[:, :, :].rearrange("p h s -> p (h s)").rearrange("p (k s) -> p k s", k=KC)
        dn = kT[:, :, :].rearrange("p h s -> p (h s)")
        sg, hh = o_sig[:, 0, :], o_sig[:, 1, :]
        hhT = hb[:, 0, :].rearrange("p (f s) -> p f s", f=FC)
        combT = hb[:, 1, 0:SEQ]

        landed = [sem(f"landed{i}") for i in range(RING)]
        x_landed = sem("x_landed")
        c_landed = sem("c_landed")
        cols_landed = sem("cols_landed")
        small_landed = sem("small_landed")
        route_landed = sem("route_landed")
        rows_landed = sem("rows_landed")
        consts = sem("consts")
        const_step = sem("const_step")
        dve_consts = sem("dve_consts")
        cT_ready, cond_ready, cols_ready, cols_copied = sem("cT_ready"), sem("cond_ready"), sem("cols_ready"), sem("cols_copied")
        ada_sum, ada_part, ada_ext = sem("ada_sum"), sem("ada_part"), sem("ada_ext")
        mod_ready, gate_row_ready = sem("mod_ready"), sem("gate_row_ready")
        xT_ready, uT_act, uT_dve = sem("xT_ready"), sem("uT_act"), sem("uT_dve")
        gates_ready, neg_ready, ln_ready, cum_ready = sem("gates_ready"), sem("neg_ready"), sem("ln_ready"), sem("cum_ready")
        aF_ready, rows_ready, bcast_ready = sem("aF_ready"), sem("rows_ready"), sem("bcast_ready")
        expm_ready, arg_ready, exp_ready = sem("expm_ready"), sem("arg_ready"), sem("exp_ready")
        proj_done, proj_act, proj_dve = sem("proj_done"), sem("proj_act"), sem("proj_dve")
        score_done, prob_ready, pv_done = sem("score_done"), sem("prob_ready"), sem("pv_done")
        hvar_ready, hrs_ready, h_ready, hT_done, hT_copied = sem("hvar_ready"), sem("hrs_ready"), sem("h_ready"), sem("hT_done"), sem("hT_copied")
        mix_done, var_ready, rs_ready, x_ready = sem("mix_done"), sem("var_ready"), sem("rs_ready"), sem("x_ready")
        logT_done, logT_copied, logit_done = sem("logT_done"), sem("logT_copied"), sem("logit_done")
        dif_ready, dexp_ready, mask_ready, pos_done = sem("dif_ready"), sem("dexp_ready"), sem("mask_ready"), sem("pos_done")
        pmax_ready, pmaxT_done, flag_ready = sem("pmax_ready"), sem("pmaxT_done"), sem("flag_ready")
        y_done = sem("y_done")
        dve_step, act_step = sem("dve_step"), sem("act_step")
        stored = sem("stored")

        class ExpertSems:
            def __init__(self, tag):
                self.disp = sem(f"disp_built{tag}")
                self.gath = sem(f"gathered{tag}")
                self.xg_act = sem(f"xg_act{tag}")
                self.xg_dve = sem(f"xg_dve{tag}")
                self.gate = sem(f"gate_done{tag}")
                self.up = sem(f"up_done{tag}")
                self.sg = sem(f"silu_ready{tag}")
                self.hh = sem(f"hidden_ready{tag}")
                self.hT = sem(f"hiddenT_done{tag}")
                self.hTc = sem(f"hiddenT_copied{tag}")
                self.cT = sem(f"combineT_done{tag}")
                self.cTc = sem(f"combineT_copied{tag}")
                self.down = sem(f"down_done{tag}")
                self.dn_act = sem(f"down_act{tag}")
                self.dn_dve = sem(f"down_dve{tag}")
                self.added = sem(f"pair_added{tag}")

        main = ExpertSems("")
        over = [ExpertSems(f"_over{l}") for l in range(DEPTH)]
        over_landed = [[sem(f"over_landed{l}_{j}") for j in range(6)] for l in range(DEPTH)]

        wg_all = w_gate.rearrange("l g e (k p) f -> (l g e) p k f", p=P)
        wu_all = w_up.rearrange("l g e (k p) f -> (l g e) p k f", p=P)
        wd_all = w_down.rearrange("l g e (k p) n -> (l g e) p k n", p=P)

        def unit_source(l, u):
            if u in ADA_UNIT:
                w, col = w_ada, ADA_UNIT.index(u) * COLS
            elif u < ADA2:
                w, col = w_in, PROJ_COL[u - PROJ]
            else:
                w, col = w_out, (u - WOUT) * COLS
            return w[l].rearrange("(k p) n -> p k n", p=P)[:, :, col:col + COLS]

        def slot(l, u):
            return (l * UNITS + u) % RING

        def arrived(eng, l, u, more=0):
            eng.wait_ge(landed[slot(l, u)], 16 * ((l * UNITS + u) // RING + 1) + 16 * more)

        def blocks_before(u):
            return [4, 8, 10, 12, 16, 20, 24][u]

        def released(eng, l, u):
            if u in ADA_UNIT:
                eng.wait_ge(ada_sum, 12 * l + ADA_UNIT.index(u) + 1)
            elif u < ADA2:
                eng.wait_ge(proj_done, NBLK * l + blocks_before(u - PROJ))
            elif u < MOE:
                eng.wait_ge(mix_done, 4 * l + 2 * (u - WOUT) + 2)
            else:
                pair, j = divmod(u - MOE, 6)
                expert_released(eng, PAIRS * l + pair, j)

        def expert_released(eng, n, j):
            if j < 2:
                eng.wait_ge(main.gate, n + 1)
            elif j < 4:
                eng.wait_ge(main.up, n + 1)
            else:
                eng.wait_ge(main.down, 2 * n + 2)

        def expert_dma(eng, l, p, j, s, signal):
            src = (wg_all, wg_all, wu_all, wu_all, wd_all, wd_all)[j]
            e = l * EXPERTS + 2 * p + j % 2
            src = src[bass.ds(e, 1)] if not isinstance(e, int) else src[e:e + 1]
            dst = ring[s][:, :, :] if j < 4 else ring[s][:, :, :].rearrange("p k n -> p (k n)").rearrange("p (k n) -> p k n", k=FC)
            eng.dma_start(dst, src.rearrange("a p k n -> p (a k) n")).then_inc(signal, 16)

        block = ctx.enter_context(nc.Block())

        @block.sync
        def _(sp):
            sp.dma_start(c_rows, c.rearrange("a (k p) -> (a k) p", p=P)).then_inc(c_landed, 16)
            for t in range(T):
                sp.dma_start(X[:, t, :], x[0, t * P:(t + 1) * P, :]).then_inc(x_landed, 16)
            for l in range(DEPTH):
                for u in range(MOE):
                    if l * UNITS + u >= RING:
                        prev = (l, u - RING) if u >= RING else (l - 1, UNITS + u - RING)
                        released(sp, *prev)
                    sp.dma_start(ring[slot(l, u)][:, :, :], unit_source(l, u)).then_inc(landed[slot(l, u)], 16)
                for j in range(6):
                    released(sp, l, MOE + j - RING)
                    expert_dma(sp, l, 0, j, slot(l, MOE + j), landed[slot(l, MOE + j)])
                with sp.Fori(1, PAIRS) as p:
                    for j in range(6):
                        expert_released(sp, PAIRS * l + p - 1, j)
                        expert_dma(sp, l, p, j, slot(l, MOE + j), landed[slot(l, MOE + j)])
                sp.wait_ge(flag_ready, l + 1)
                more = sp.value_load(flag[0:1, l:l + 1])
                with sp.If(more != 0):
                    sp.wait_ge(main.down, 2 * PAIRS * (l + 1))
                    with sp.Fori(0, ROUNDS - 1) as r:
                        with sp.Fori(0, PAIRS) as p:
                            for j in range(6):
                                sp.wait_ge(over[l].down, 2 * (r * PAIRS + p))
                                expert_dma(sp, l, p, j, slot(l, MOE + j), over_landed[l][j])
                    sp.wait_ge(over[l].down, 2 * (ROUNDS - 1) * PAIRS)
            for t in range(T):
                sp.wait_ge(x_ready, 2 * T * (DEPTH - 1) + T + t + 1)
                sp.dma_start(out[0, t * P:(t + 1) * P, :], X[:, t, :]).then_inc(stored, 16)
            sp.wait_ge(stored, 16 * T)

        @block.gpsimd
        def _(pool):
            def select(t, pattern, base, cm, op, fill):
                return pool.affine_select(out=t, in_=t, compare_op=op, fill=fill, base=base,
                                          pattern=pattern, channel_multiplier=cm)

            def load_rows(l, which):
                g, b = ((ln1_g, ln1_b), (ln2_g, ln2_b))[which]
                gt = (2, 5)[which]
                pool.dma_start(gate_row[:, which, :], b_ada[l, gt * D:(gt + 1) * D].partition_broadcast(P)).then_inc(rows_landed, 16)
                pool.dma_start(ln_g[:, which, :], g[l].partition_broadcast(P)).then_inc(rows_landed, 16)
                pool.dma_start(ln_b[:, which, :], b[l].partition_broadcast(P)).then_inc(rows_landed, 16)
                if which == 0:
                    pool.dma_start(mh_w[:, :], mh_norm_w[l].partition_broadcast(P)).then_inc(rows_landed, 16)

            pool.memset(ident[:, :], 0.0).then_inc(const_step, 1)
            pool.memset(partials[:, :], 0.0).then_inc(const_step, 1)
            pool.memset(causal[:, :], 0.0).then_inc(const_step, 1)
            pool.memset(before[:, :], 1.0).then_inc(const_step, 1)
            pool.memset(ones[:, :], 1.0).then_inc(const_step, 1)
            pool.memset(pick_i[:, :], 0.0).then_inc(const_step, 1)
            pool.memset(pick_f[:, :], 0.0).then_inc(const_step, 1)
            pool.memset(pick_negf[:, :], 0.0).then_inc(const_step, 1)
            pool.memset(head_row[:, :, :], 0.0).then_inc(const_step, 1)
            pool.wait_ge(const_step, 9)
            select(ident[:, :], [[-1, P]], 0, 1, ALU.not_equal, 1.0).then_inc(const_step, 1)
            for r in range(4):
                pool.wait_ge(const_step, 10 + r)
                pool.memset(partials[32 * r:32 * r + 1, :], 1.0).then_inc(const_step, 1)
            pool.wait_ge(const_step, 14)
            select(causal[:, 0:SEQ], [[1, SEQ]], 0, -1, ALU.is_ge, MASKED).then_inc(const_step, 1)
            select(causal[:, SEQ:SEQ + P], [[1, P]], 0, -1, ALU.is_ge, MASKED).then_inc(const_step, 1)
            select(before[:, :], [[1, P]], 0, -1, ALU.is_gt, 0.0).then_inc(const_step, 1)
            select(pick_i[:, :], [[-1, HEADS]], 0, 1, ALU.not_equal, 1.0).then_inc(const_step, 1)
            select(pick_f[:, :], [[-1, HEADS]], -HEADS, 1, ALU.not_equal, 1.0).then_inc(const_step, 1)
            select(pick_negf[:, :], [[-1, HEADS]], -HEADS, 1, ALU.not_equal, -1.0).then_inc(const_step, 1)
            select(head_row[:, :, :], [[-1, HEADS], [0, P]], 0, 1, ALU.not_equal, 1.0).then_inc(const_step, 1)
            pool.iota(slots[:, :], pattern=[[1, CAP]], base=0, channel_multiplier=0,
                      allow_small_or_imprecise_dtypes=True).then_inc(const_step, 1)
            pool.iota(prefer[:, :], pattern=[[-1, G]], base=G, channel_multiplier=0,
                      allow_small_or_imprecise_dtypes=True).then_inc(const_step, 1)
            pool.wait_ge(const_step, 23)
            pool.memset(tmp[:, 0:1], 0.0).then_inc(consts, 1)

            for l in range(DEPTH):
                if l:
                    pool.wait_ge(x_ready, 2 * T * (l - 1) + T)
                load_rows(l, 0)
                if l:
                    pool.wait_ge(x_ready, 2 * T * l)
                load_rows(l, 1)

        @block.tensor
        def _(pe):
            def ada_unit(l, i):
                n = 12 * l + i
                if i >= 2:
                    pe.wait_ge(ada_part, n - 1)
                arrived(pe, l, ADA_UNIT[i])
                w = ring[slot(l, ADA_UNIT[i])]
                for kc in range(KC):
                    g = kc % 4
                    last = pe.matmul(bank[4 + i % 2][32 * g:32 * g + 32, :], cond[:, kc, :], w[:, kc, :],
                                     start=(kc < 4), stop=(kc >= 4), tile_position=(0, 32 * g))
                last.then_inc(ada_sum, 1)

            def ada_extract(l, i):
                pe.wait_ge(ada_part, 12 * l + i + 1)
                if i // 2 in (2, 5):
                    last = pe.matmul(bank[(7, 5)[i % 2]][:, :], partials[:, :], part[:, i % 2, :], start=True, stop=True)
                else:
                    for q in range(4):
                        last = pe.matmul(bank[6][:, 4 * i + q:4 * i + q + 1], part[:, i % 2, q * P:(q + 1) * P],
                                         partials[:, 0:1], start=True, stop=True)
                last.then_inc(ada_ext, 1)

            def ada_units(l, first, n):
                for i in range(first, first + n):
                    ada_unit(l, i)
                    if i > first:
                        ada_extract(l, i - 1)
                ada_extract(l, first + n - 1)

            def transpose_x():
                for kc in range(KC):
                    for t in range(T):
                        o = (kc % 2) * SEQ + t * P
                        last = pe.transpose(bank[kc // 2][:, o:o + P], X[:, t, kc * P:(kc + 1) * P], ident[:, :])
                    if kc % 2:
                        last.then_inc(xT_ready, 1)

            def wait_block(l, b):
                if b >= 4:
                    if b - 4 < 16:
                        pe.wait_ge(proj_act, 16 * l + b - 3)
                    else:
                        pe.wait_ge(proj_dve, 8 * l + b - 19)

            def proj_channels(l, u, b0):
                arrived(pe, l, PROJ + u)
                w = ring[slot(l, PROJ + u)]
                for q in range(4):
                    wait_block(l, b0 + q)
                    for kc in range(KC):
                        last = pe.matmul(bank[4 + (b0 + q) % 4][:, 0:SEQ], w[:, kc, q * P:(q + 1) * P],
                                         uT[:, kc, :], start=(kc == 0), stop=(kc == KC - 1))
                    last.then_inc(proj_done, 1)

            def proj_tokens(l, u, b0):
                arrived(pe, l, PROJ + u)
                w = ring[slot(l, PROJ + u)]
                for t in range(T):
                    wait_block(l, b0 + t)
                    for kc in range(KC):
                        last = pe.matmul(bank[4 + (b0 + t) % 4][:, :], uT[:, kc, t * P:(t + 1) * P],
                                         w[:, kc, :], start=(kc == 0), stop=(kc == KC - 1))
                    last.then_inc(proj_done, 1)

            def gather(S, n, b):
                pe.wait_ge(S.disp, n + 1)
                for kc in range(KC):
                    for t in range(T):
                        last = pe.matmul(bank[6 + kc // 4][:, (kc % 4) * P:(kc % 4 + 1) * P],
                                         X[:, t, kc * P:(kc + 1) * P], disp[b][:, t, :],
                                         start=(t == 0), stop=(t == T - 1))
                    if kc % 4 == 3:
                        last.then_inc(S.gath, 1)

            def gate_up(bk, wa, wb, done):
                for kc in range(KC):
                    for j, w in enumerate((wa, wb)):
                        last = pe.matmul(bank[bk][CAP * j:CAP * (j + 1), :], xg[:, kc, CAP * j:CAP * (j + 1)],
                                         w[:, kc, :], start=(kc == 0), stop=(kc == KC - 1), tile_position=(0, CAP * j))
                last.then_inc(done, 1)

            def hidden_T(S, n):
                pe.wait_ge(S.hh, n + 1)
                for f in range(FC):
                    last = pe.transpose(bank[6][:, f * P:(f + 1) * P], hh[:, f * P:(f + 1) * P], ident[:, :])
                last.then_inc(S.hT, 1)

            def combine_T(S, b):
                for t in range(T):
                    last = pe.transpose(bank[7][:, t * P:(t + 1) * P], dispw[b][:, t, :], ident[:, :])
                last.then_inc(S.cT, 1)

            def down(S, n, sa, sb_):
                wa, wb = (ring[s][:, :, :].rearrange("p k n -> p (k n)").rearrange("p (k n) -> p k n", k=FC) for s in (sa, sb_))
                for half in range(2):
                    if half == 0:
                        pe.wait_ge(S.hTc, n + 1)
                    else:
                        pe.wait_ge(S.cTc, n + 1)
                    for f in range(FC):
                        for j, w in enumerate((wa, wb)):
                            last = pe.matmul(bank[6 + half][CAP * j:CAP * (j + 1), :], hhT[:, f, CAP * j:CAP * (j + 1)],
                                             w[:, f, half * COLS:(half + 1) * COLS],
                                             start=(f == 0), stop=(f == FC - 1), tile_position=(0, CAP * j))
                    last.then_inc(S.down, 1)

            def combine(S, n):
                pe.wait_ge(S.dn_act, n + 1)
                pe.wait_ge(S.dn_dve, n + 1)
                pe.wait_ge(S.cTc, n + 1)
                for t in range(T):
                    for half in range(2):
                        last = pe.matmul(bank[2 * t + half][:, :], combT[:, t * P:(t + 1) * P],
                                         dn[:, half * COLS:(half + 1) * COLS], start=False, stop=False,
                                         skip_group_check=True)
                last.then_inc(S.added, 1)

            def pair(l, p, b, first=False, final=False):
                n = PAIRS * l + p
                turn = p
                s = [slot(l, MOE + j) for j in range(6)]
                for j in (0, 1):
                    arrived(pe, l, MOE + j, turn)
                pe.wait_ge(main.xg_act, n + 1)
                pe.wait_ge(main.xg_dve, n + 1)
                gate_up(4, ring[s[0]], ring[s[1]], main.gate)
                if not first:
                    combine(main, n - 1)
                for j in (2, 3):
                    arrived(pe, l, MOE + j, turn)
                gate_up(5, ring[s[2]], ring[s[3]], main.up)
                if not final:
                    gather(main, n + 1, 1 - b)
                    pe.wait_ge(main.xg_act, n + 2)
                hidden_T(main, n)
                if not final:
                    pe.wait_ge(main.xg_dve, n + 2)
                combine_T(main, b)
                for j in (4, 5):
                    arrived(pe, l, MOE + j, turn)
                down(main, n, s[4], s[5])

            pe.wait_ge(consts, 1)
            pe.wait_ge(c_landed, 16)
            pe.transpose(bank[7][:, 256:256 + KC], c_rows, ident[0:KC, 0:KC]).then_inc(cT_ready, 1)
            pe.wait_ge(cond_ready, 1)

            for l in range(DEPTH):
                ada_units(l, 0, 4)
                if l == 0:
                    pe.wait_ge(cols_landed, 16 * 2 * DEPTH)
                    for i in range(DEPTH):
                        pe.transpose(bank[7][:, 64 * i:64 * i + NMOD], b_ada_rows[:, i, :], ident[0:NMOD, 0:NMOD])
                        last = pe.transpose(bank[7][:, 128 + 16 * i:128 + 16 * i + 3 * CH], w_conv_rows[:, i, :],
                                            ident[0:3 * CH, 0:3 * CH])
                    last.then_inc(cols_ready, 1)
                    pe.wait_ge(x_landed, 16 * T)
                else:
                    pe.wait_ge(x_ready, 2 * T * l)
                transpose_x()
                pe.wait_ge(uT_act, 8 * l + 4)
                pe.wait_ge(uT_dve, 8 * l + 4)
                pe.wait_ge(small_landed, 16 * 4 * DEPTH)
                for kc in range(KC):
                    last = pe.matmul(bank[3][0:8, 0:SEQ], w_gates_sb[:, l, kc, :], uT[:, kc, :],
                                     start=(kc == 0), stop=(kc == KC - 1))
                last.then_inc(gates_ready, 1)
                proj_channels(l, 0, 0)
                pe.wait_ge(cum_ready, l + 1)
                pe.matmul(bank[2][0:HEADS, 0:SEQ], pick_i[:, :], gate_pre, start=True, stop=False)
                pe.matmul(bank[2][0:HEADS, 0:SEQ], pick_negf[:, :], cums[0][:, P:P + SEQ], start=False, stop=True)
                pe.matmul(bank[2][0:HEADS, SEQ:2 * SEQ], pick_f[:, :], cums[0][:, P:P + SEQ],
                          start=True, stop=True).then_inc(aF_ready, 1)
                proj_channels(l, 1, 4)
                pe.wait_ge(rows_ready, l + 1)
                for t in range(T):
                    pe.transpose(bank[3][:, 8 * t:8 * t + HEADS], a_row[:, t * P:(t + 1) * P], ident[0:HEADS, 0:HEADS])
                    pe.transpose(bank[2][:, 8 * t:8 * t + HEADS], neg_m[:, t * P:(t + 1) * P], ident[0:HEADS, 0:HEADS])
                for h in range(HEADS):
                    last = pe.matmul(bank[h // 2][:, (h % 2) * SEQ:(h % 2 + 1) * SEQ], head_row[:, h, :],
                                     neg_g, start=True, stop=True)
                last.then_inc(bcast_ready, 1)
                proj_tokens(l, 2, 8)
                pe.wait_ge(proj_act, 16 * l + 8)
                pe.wait_ge(arg_ready, HEADS * (l + 1))
                pe.wait_ge(expm_ready, l + 1)
                for h in range(HEADS):
                    pe.matmul(bank[h][:, 0:SEQ], kT[:, h, 0:P], qT[:, h, :], start=True, stop=True)
                    pe.matmul(bank[h][:, SEQ:SEQ + P], kT[:, h, P:SEQ], qT[:, h, P:SEQ],
                              start=True, stop=True).then_inc(score_done, 1)
                proj_tokens(l, 3, 10)
                proj_channels(l, 4, 12)
                pe.wait_ge(proj_act, 16 * l + 10)
                for h in range(HEADS):
                    pe.wait_ge(prob_ready, HEADS * l + h + 1)
                    pe.matmul(bank[h][:, 0:DK + 1], expo[:, h, 0:P], v_ext[:, 0, h, :], start=True, stop=True)
                    pe.matmul(bank[h][:, DK + 1:2 * DK + 2], expo[:, h, P:SEQ], v_ext[:, 0, h, :], start=True, stop=False)
                    pe.matmul(bank[h][:, DK + 1:2 * DK + 2], expo[:, h, SEQ:SEQ + P], v_ext[:, 1, h, :],
                              start=False, stop=True).then_inc(pv_done, 1)
                proj_channels(l, 5, 16)
                proj_channels(l, 6, 20)
                pe.wait_ge(proj_dve, 8 * l + 8)
                ada_units(l, 4, 2)
                pe.wait_ge(h_ready, l + 1)
                pe.wait_ge(gate_row_ready, 4 * l + 2)
                for h in range(HEADS):
                    for t in range(T):
                        o = (h % 2) * SEQ + t * P
                        last = pe.transpose(bank[4 + h // 2][:, o:o + P], hb[:, t, h * DK:(h + 1) * DK], ident[:, :])
                    if h % 2:
                        last.then_inc(hT_done, 1)
                pe.wait_ge(hT_copied, 2 * (l + 1))
                for half in range(2):
                    arrived(pe, l, WOUT + half)
                    w = ring[slot(l, WOUT + half)]
                    for t in range(T):
                        for kc in range(KC):
                            last = pe.matmul(bank[2 * t + half][:, :], mixT[:, kc, t * P:(t + 1) * P], w[:, kc, :],
                                             start=(kc == 0), stop=(kc == KC - 1))
                        last.then_inc(mix_done, 1)
                ada_units(l, 6, 4)
                pe.wait_ge(x_ready, 2 * T * l + T)
                transpose_x()
                pe.wait_ge(uT_act, 8 * l + 8)
                pe.wait_ge(uT_dve, 8 * l + 8)
                pe.wait_ge(route_landed, 16 * 2 * DEPTH)
                for kc in range(KC):
                    last = pe.matmul(bank[6][0:G + EXPERTS, 0:SEQ], w_route_sb[:, l, kc, :], uT[:, kc, :],
                                     start=(kc == 0), stop=(kc == KC - 1))
                last.then_inc(logT_done, 1)
                for b in range(4):
                    pe.matmul(bank[b][:, :], zeros[:, 0:P], zeros[:, :], start=True, stop=False, skip_group_check=True)
                pe.wait_ge(logT_copied, l + 1)
                for t in range(T):
                    last = pe.transpose(bank[6][:, 32 * t:32 * t + G + EXPERTS], logT[:, t * P:(t + 1) * P],
                                        ident[0:G + EXPERTS, 0:G + EXPERTS])
                last.then_inc(logit_done, 1)
                ada_unit(l, 10)
                ada_unit(l, 11)
                pe.wait_ge(mask_ready, l + 1)
                pe.matmul(bank[6][:, 0:EXPERTS], before[:, :], mask[:, 0, :], start=True, stop=True)
                pe.matmul(bank[6][:, EXPERTS:2 * EXPERTS], ones[:, :], mask[:, 0, :], start=True, stop=False)
                pe.matmul(bank[6][:, EXPERTS:2 * EXPERTS], before[:, :], mask[:, 1, :],
                          start=False, stop=True).then_inc(pos_done, 1)
                ada_extract(l, 10)
                ada_extract(l, 11)
                pe.wait_ge(pmax_ready, l + 1)
                pe.transpose(bank[4][0:1, 0:P], pmax[:, :], ident[:, :]).then_inc(pmaxT_done, 1)

                pe.wait_ge(gate_row_ready, 4 * l + 4)
                gather(main, PAIRS * l, 0)
                pe.wait_ge(flag_ready, l + 1)
                pair(l, 0, 0, first=True)
                with pe.Fori(0, (PAIRS - 2) // 2) as i:
                    pair(l, 2 * i + 1, 1)
                    pair(l, 2 * i + 2, 0)
                pair(l, PAIRS - 1, 1, final=True)
                combine(main, PAIRS * (l + 1) - 1)
                more = pe.value_load(flag[0:1, l:l + 1])
                with pe.If(more != 0):
                    S = over[l]
                    s = [slot(l, MOE + j) for j in range(6)]
                    with pe.Fori(0, ROUNDS - 1) as r:
                        with pe.Fori(0, PAIRS) as p:
                            n = r * PAIRS + p
                            gather(S, n, 0)
                            pe.wait_ge(S.xg_act, n + 1)
                            pe.wait_ge(S.xg_dve, n + 1)
                            for j in range(2):
                                pe.wait_ge(over_landed[l][j], 16 * n + 16)
                            gate_up(4, ring[s[0]], ring[s[1]], S.gate)
                            for j in range(2, 4):
                                pe.wait_ge(over_landed[l][j], 16 * n + 16)
                            gate_up(5, ring[s[2]], ring[s[3]], S.up)
                            hidden_T(S, n)
                            combine_T(S, 0)
                            for j in range(4, 6):
                                pe.wait_ge(over_landed[l][j], 16 * n + 16)
                            down(S, n, s[4], s[5])
                            combine(S, n)
                pe.matmul(bank[0][:, :], zeros[:, 0:P], zeros[:, :], start=False, stop=True,
                          skip_group_check=True).then_inc(y_done, 1)

        @block.scalar
        def _(act):
            steps = [0]

            def link(ins):
                steps[0] += 1
                ins.then_inc(act_step, 1)
                act.wait_ge(act_step, steps[0])

            def ada_copies(l, first, n):
                for i in range(first, first + n):
                    act.wait_ge(ada_sum, 12 * l + i + 1)
                    if 12 * l + i >= 2:
                        act.wait_ge(ada_ext, 12 * l + i - 1)
                    act.activation(part[:, i % 2, :], bank[4 + i % 2][:, :], ACT.Copy).then_inc(ada_part, 1)

            def modulate(l, which):
                for kc in (2, 3, 6, 7):
                    act.wait_ge(xT_ready, 8 * l + 4 * which + kc // 2 + 1)
                    act.activation(uT[:, kc, :], bank[kc // 2][:, (kc % 2) * SEQ:(kc % 2 + 1) * SEQ], ACT.Identity,
                                   bias=mod[:, 2 * which, kc:kc + 1], scale=mod[:, 2 * which + 1, kc:kc + 1]).then_inc(uT_act, 1)

            def rsqrt(n, ready, value, done):
                act.wait_ge(ready, value)
                link(act.activation(lnv[:, 0:n], var[:, 0:n], ACT.Ln))
                act.activation(rstd[:, 0:n], lnv[:, 0:n], ACT.Exp, scale=-0.5).then_inc(done, 1)

            def xg_half(S, n):
                act.wait_ge(S.gath, 2 * n + 1)
                for kc in range(4):
                    last = act.activation(xg[:, kc, :], bank[6][:, kc * P:(kc + 1) * P], ACT.Identity,
                                          bias=mod[:, 2, kc:kc + 1], scale=mod[:, 3, kc:kc + 1])
                last.then_inc(S.xg_act, 1)

            def silu(S, n):
                act.wait_ge(S.gate, n + 1)
                act.wait_ge(S.hh, n)
                act.activation(sg, bank[4][:, :], ACT.Silu).then_inc(S.sg, 1)

            def copies(S, n):
                act.wait_ge(S.hT, n + 1)
                act.activation(hb[:, 0, :], bank[6][:, :], ACT.Copy).then_inc(S.hTc, 1)
                act.wait_ge(S.down, 2 * n + 1)
                act.activation(dn[:, 0:COLS], bank[6][:, :], ACT.Copy).then_inc(S.dn_act, 1)

            for l in range(DEPTH):
                act.dma_start(b_ada_rows[:, l, :], b_ada[l].rearrange("(k p) -> k p", p=P)).then_inc(cols_landed, 16)
                act.dma_start(w_conv_rows[:, l, :], w_conv[l].rearrange("k (c p) -> (k c) p", p=P)).then_inc(cols_landed, 16)
            for l in range(DEPTH):
                act.dma_start(b_gates_col[:, l:l + 1], b_gates[l].rearrange("(k a) -> k a", a=1)).then_inc(small_landed, 16)
                act.dma_start(w_gates_sb[:, l, :, :], w_in[l].rearrange("(k p) n -> p k n", p=P)[:, :, COL_GATES:COL_GATES + 8]).then_inc(small_landed, 16)
                act.dma_start(b_route_col[0:G, l:l + 1], b_grp[l].rearrange("(k a) -> k a", a=1)).then_inc(small_landed, 16)
                act.dma_start(b_route_col[G:G + EXPERTS, l:l + 1], b_router[l].rearrange("(k a) -> k a", a=1)).then_inc(small_landed, 16)
            act.wait_ge(cT_ready, 1)
            for kc in range(KC):
                last = act.activation(cond[:, kc, :], bank[7][:, 256 + kc:257 + kc].to_broadcast([P, 32]), ACT.Silu)
            last.then_inc(cond_ready, 1)

            for l in range(DEPTH):
                ada_copies(l, 0, 4)
                if l == 0:
                    for i in range(DEPTH):
                        act.dma_start(w_route_sb[:, i, :, 0:G], w_grp[i].rearrange("(k p) n -> p k n", p=P)).then_inc(route_landed, 16)
                        act.dma_start(w_route_sb[:, i, :, G:G + EXPERTS], w_router[i].rearrange("(k p) n -> p k n", p=P)).then_inc(route_landed, 16)
                act.wait_ge(mod_ready, 2 * l + 1)
                modulate(l, 0)
                act.wait_ge(neg_ready, l + 1)
                link(act.activation(gate_ln, gate_neg, ACT.Exp))
                act.activation(gate_ln, gate_ln, ACT.Ln, bias=1.0).then_inc(ln_ready, 1)
                for b in range(8):
                    act.wait_ge(proj_done, NBLK * l + b + 1)
                    act.activation((qT, kT)[b // 4][:, b % 4, :], bank[4 + b % 4][:, 0:SEQ], ACT.Copy).then_inc(proj_act, 1)
                act.wait_ge(bcast_ready, l + 1)
                act.activation(exp_neg_m[:, :, :], bank[2][:, 0:16].rearrange("p (t c) -> p t c", t=T)[:, :, 0:HEADS],
                               ACT.Exp).then_inc(expm_ready, 1)
                for h in range(HEADS):
                    act.wait_ge(arg_ready, HEADS * l + h + 1)
                    act.activation(expo[:, h, :], expo[:, h, :], ACT.Exp).then_inc(exp_ready, 1)
                for t in range(T):
                    act.wait_ge(proj_done, NBLK * l + 9 + t)
                    if t == 0:
                        act.wait_ge(dve_consts, 1)
                    act.activation(v_ext[:, t, :, 0:DK], bank[4 + t][:, :].rearrange("p (h d) -> p h d", h=HEADS),
                                   ACT.Copy).then_inc(proj_act, 1)
                for t in range(T):
                    act.wait_ge(proj_done, NBLK * l + 11 + t)
                    act.activation(o_sig[:, t, :], bank[6 + t][:, :], ACT.Exp, scale=-1.0).then_inc(proj_act, 1)
                for q in range(CH):
                    act.wait_ge(proj_done, NBLK * l + 13 + q)
                    act.activation(ccT[:, q, :], bank[4 + q][:, 0:SEQ], ACT.Copy).then_inc(proj_act, 1)
                rsqrt(T * HEADS, hvar_ready, l + 1, hrs_ready)
                ada_copies(l, 4, 2)
                for b in range(2):
                    act.wait_ge(hT_done, 2 * l + b + 1)
                    act.activation(mixT[:, 2 * b:2 * b + 2, :], bank[4 + b][:, :].rearrange("p (h s) -> p h s", h=2),
                                   ACT.Copy).then_inc(hT_copied, 1)
                ada_copies(l, 6, 4)
                rsqrt(T, var_ready, 2 * l + 1, rs_ready)
                act.wait_ge(mod_ready, 2 * l + 2)
                modulate(l, 1)
                act.wait_ge(dif_ready, l + 1)
                act.activation(dexp[:, :, :], dif[:, :, :], ACT.Exp).then_inc(dexp_ready, 1)
                ada_copies(l, 10, 2)
                xg_half(main, PAIRS * l)

                def pair(p, final=False):
                    n = PAIRS * l + p
                    silu(main, n)
                    if not final:
                        xg_half(main, n + 1)
                    copies(main, n)

                pair(0)
                with act.Fori(0, PAIRS - 2) as p:
                    pair(p + 1)
                pair(PAIRS - 1, final=True)
                act.wait_ge(flag_ready, l + 1)
                more = act.value_load(flag[0:1, l:l + 1])
                with act.If(more != 0):
                    with act.Fori(0, ROUNDS - 1) as r:
                        with act.Fori(0, PAIRS) as p:
                            xg_half(over[l], r * PAIRS + p)
                            silu(over[l], r * PAIRS + p)
                            copies(over[l], r * PAIRS + p)
                rsqrt(T, var_ready, 2 * l + 2, rs_ready)

        @block.vector
        def _(dve):
            steps = [0]

            def link(ins):
                steps[0] += 1
                ins.then_inc(dve_step, 1)
                dve.wait_ge(dve_step, steps[0])

            def modulate(l, which):
                for kc in (0, 1, 4, 5):
                    dve.wait_ge(xT_ready, 8 * l + 4 * which + kc // 2 + 1)
                    dve.tensor_scalar(uT[:, kc, :], bank[kc // 2][:, (kc % 2) * SEQ:(kc % 2 + 1) * SEQ],
                                      mod[:, 2 * which + 1, kc:kc + 1], mod[:, 2 * which, kc:kc + 1],
                                      ALU.mult, ALU.add).then_inc(uT_dve, 1)

            def newton(n, ready, value):
                dve.wait_ge(ready, value)
                link(dve.tensor_tensor(nt[:, 0:n], rstd[:, 0:n], rstd[:, 0:n], ALU.mult))
                link(dve.tensor_tensor(nt[:, 0:n], nt[:, 0:n], var[:, 0:n], ALU.mult))
                link(dve.tensor_scalar(nt[:, 0:n], nt[:, 0:n], -0.5, 1.5, ALU.mult, ALU.add))
                link(dve.tensor_tensor(rstd[:, 0:n], rstd[:, 0:n], nt[:, 0:n], ALU.mult))

            def gate_rows(l, which, i0):
                for half in range(2):
                    dve.wait_ge(ada_ext, 12 * l + i0 + half + 1)
                    cols = slice(half * COLS, (half + 1) * COLS)
                    dve.scalar_tensor_tensor(out=gate_row[:, which, cols], in0=bank[(7, 5)[half]][:, :], scalar=1.0,
                                             in1=gate_row[:, which, cols], op0=ALU.add, op1=ALU.add).then_inc(gate_row_ready, 1)

            def shift_scale(l):
                dve.wait_ge(ada_ext, 12 * l + 10)
                dve.tensor_tensor(mod[:, 2, :], bank[6][:, 3 * KC:4 * KC], b_ada_col[:, l, 3 * KC:4 * KC], ALU.add)
                dve.scalar_tensor_tensor(out=mod[:, 3, :], in0=bank[6][:, 4 * KC:5 * KC], scalar=1.0,
                                         in1=b_ada_col[:, l, 4 * KC:5 * KC], op0=ALU.add, op1=ALU.add).then_inc(mod_ready, 1)

            def residual_norm(l, which, between=None):
                for half in range(2):
                    for t in range(T):
                        if which == 0:
                            dve.wait_ge(mix_done, 4 * l + 2 * half + t + 1)
                        elif half == 0 and t == 0:
                            dve.wait_ge(y_done, l + 1)
                        cols = slice(half * COLS, (half + 1) * COLS)
                        link(dve.tensor_tensor(tmp[:, :], bank[2 * t + half][:, :], gate_row[:, which, cols], ALU.mult))
                        link(dve.scalar_tensor_tensor(out=X[:, t, cols], in0=X[:, t, cols], scalar=ALPHA,
                                                      in1=tmp[:, :], op0=ALU.mult, op1=ALU.add))
                        link(dve.bn_stats(stats[:, t, half, :], X[:, t, cols]))
                for t in range(T):
                    last = dve.bn_aggr(mv[:, t, :], stats[:, t, :, :].rearrange("p a b -> p (a b)"))
                link(last)
                dve.tensor_scalar(var[:, 0:T], mv[:, :, 1], EPS, None, ALU.add).then_inc(var_ready, 1)
                newton(T, rs_ready, 2 * l + which + 1)
                for t in range(T):
                    link(dve.tensor_scalar(X[:, t, :], X[:, t, :], mv[:, t, 0:1], rstd[:, t:t + 1], ALU.subtract, ALU.mult))
                    link(dve.tensor_tensor(X[:, t, :], X[:, t, :], ln_g[:, which, :], ALU.mult))
                    dve.tensor_tensor(X[:, t, :], X[:, t, :], ln_b[:, which, :], ALU.add).then_inc(x_ready, 1)
                if between:
                    between()
                    dve.wait_ge(mod_ready, 2 * l + 2)

            def first_of(value, biggest, chosen):
                link(dve.tensor_tensor(sc[:, :, :], value, biggest.to_broadcast([P, T, E]), ALU.is_equal))
                link(dve.tensor_tensor(sc[:, :, :], sc[:, :, :], prefer[:, :].unsqueeze(1).to_broadcast([P, T, E]), ALU.mult))
                link(dve.tensor_reduce(scm[:, :, :], sc[:, :, :], AX.X, ALU.max))
                link(dve.tensor_tensor(chosen, sc[:, :, :], scm[:, :, :].to_broadcast([P, T, E]), ALU.is_equal))

            def build(S, e0, b):
                for t in range(T):
                    for j in range(2):
                        e = e0 + j
                        col = slice(e, e + 1) if isinstance(e, int) else bass.ds(e, 1)
                        dve.tensor_scalar(disp[b][:, t, CAP * j:CAP * (j + 1)], slots[:, :], pos[:, t, col], None, ALU.is_equal)
                        last = dve.tensor_scalar(dispw[b][:, t, CAP * j:CAP * (j + 1)], slots[:, :], pos[:, t, col],
                                                 comb[:, t, col], ALU.is_equal, ALU.mult)
                last.then_inc(S.disp, 1)

            def xg_half(S, n):
                dve.wait_ge(S.gath, 2 * n + 2)
                for kc in range(4, KC):
                    last = dve.tensor_scalar(xg[:, kc, :], bank[7][:, (kc - 4) * P:(kc - 3) * P], mod[:, 3, kc:kc + 1],
                                             mod[:, 2, kc:kc + 1], ALU.mult, ALU.add)
                last.then_inc(S.xg_dve, 1)

            def hidden(S, n):
                dve.wait_ge(S.sg, n + 1)
                dve.wait_ge(S.up, n + 1)
                dve.wait_ge(S.hT, n)
                dve.tensor_tensor(hh, sg, bank[5][:, :], ALU.mult).then_inc(S.hh, 1)

            def combine_copy(S, n):
                dve.wait_ge(S.cT, n + 1)
                dve.tensor_copy(combT, bank[7][:, 0:SEQ]).then_inc(S.cTc, 1)

            def down_copy(S, n):
                dve.wait_ge(S.down, 2 * n + 2)
                dve.tensor_copy(dn[:, COLS:2 * COLS], bank[7][:, :]).then_inc(S.dn_dve, 1)

            dve.memset(zeros[:, :], 0.0)
            dve.memset(v_ext[:, :, :, DK:DK + 1], 1.0)
            dve.memset(zT[:, :, 0:2], 0.0)
            for i in range(2):
                dve.memset(cums[i][:, 0:P], 0.0)
                last = dve.memset(maxs[i][:, 0:P], 0.0)
            last.then_inc(dve_consts, 1)
            dve.wait_ge(dve_consts, 1)
            dve.wait_ge(consts, 1)

            for l in range(DEPTH):
                if l == 0:
                    dve.wait_ge(cols_ready, 1)
                    for i in range(DEPTH):
                        dve.tensor_copy(b_ada_col[:, i, :], bank[7][:, 64 * i:64 * i + NMOD])
                        last = dve.tensor_copy(w_conv_col[:, i, :], bank[7][:, 128 + 16 * i:128 + 16 * i + 3 * CH])
                    last.then_inc(cols_copied, 1)
                    dve.wait_ge(cols_copied, 1)
                dve.wait_ge(ada_ext, 12 * l + 4)
                dve.tensor_tensor(mod[:, 0, :], bank[6][:, 0:KC], b_ada_col[:, l, 0:KC], ALU.add)
                last = dve.scalar_tensor_tensor(out=mod[:, 1, :], in0=bank[6][:, KC:2 * KC], scalar=1.0,
                                                in1=b_ada_col[:, l, KC:2 * KC], op0=ALU.add, op1=ALU.add)
                last.then_inc(mod_ready, 1)
                dve.wait_ge(mod_ready, 2 * l + 1)
                modulate(l, 0)
                dve.wait_ge(gates_ready, l + 1)
                dve.wait_ge(small_landed, 16 * 4 * DEPTH)
                link(dve.tensor_scalar(gate_pre, bank[3][0:8, 0:SEQ], b_gates_col[:, l:l + 1], None, ALU.add))
                dve.scalar_tensor_tensor(out=gate_neg, in0=gate_pre, scalar=-1.0, in1=gate_pre,
                                         op0=ALU.mult, op1=ALU.min).then_inc(neg_ready, 1)
                dve.wait_ge(ln_ready, l + 1)
                link(dve.scalar_tensor_tensor(out=cums[0][:, P:P + SEQ], in0=gate_pre, scalar=0.0,
                                              in1=gate_ln, op0=ALU.min, op1=ALU.subtract))
                for i in range(8):
                    s, a, b = 1 << i, cums[i % 2], cums[1 - i % 2]
                    ins = dve.tensor_tensor(b[:, P:P + SEQ], a[:, P:P + SEQ], a[:, P - s:P - s + SEQ], ALU.add)
                    if i < 7:
                        link(ins)
                ins.then_inc(cum_ready, 1)
                dve.wait_ge(aF_ready, l + 1)
                dve.tensor_copy(a_row, bank[2][0:HEADS, 0:SEQ])
                link(dve.tensor_copy(maxs[0][:, P:P + SEQ], bank[2][0:HEADS, 0:SEQ]))
                for i in range(8):
                    s, a, b = 1 << i, maxs[i % 2], maxs[1 - i % 2]
                    link(dve.tensor_tensor(b[:, P:P + SEQ], a[:, P:P + SEQ], a[:, P - s:P - s + SEQ], ALU.max))
                link(dve.tensor_scalar(maxs[0][:, P:P + SEQ], maxs[0][:, P:P + SEQ], 0.0, None, ALU.max))
                dve.tensor_scalar(neg_g, maxs[0][:, P:P + SEQ], -1.0, None, ALU.mult)
                dve.scalar_tensor_tensor(out=neg_m, in0=bank[2][0:HEADS, SEQ:2 * SEQ], scalar=-1.0,
                                         in1=maxs[0][:, P:P + SEQ], op0=ALU.mult, op1=ALU.subtract).then_inc(rows_ready, 1)
                dve.wait_ge(bcast_ready, l + 1)
                link(dve.tensor_copy(a_col[:, :, :], bank[3][:, 0:16].rearrange("p (t c) -> p t c", t=T)[:, :, 0:4]))
                for h in range(HEADS):
                    g = bank[h // 2][:, (h % 2) * SEQ:(h % 2 + 1) * SEQ]
                    dve.scalar_tensor_tensor(out=expo[:, h, 0:SEQ], in0=g, scalar=a_col[:, 0, h:h + 1],
                                             in1=causal[:, 0:SEQ], op0=ALU.add, op1=ALU.add)
                    dve.scalar_tensor_tensor(out=expo[:, h, SEQ:SEQ + P], in0=g[:, P:SEQ], scalar=a_col[:, 1, h:h + 1],
                                             in1=causal[:, SEQ:SEQ + P], op0=ALU.add, op1=ALU.add).then_inc(arg_ready, 1)
                for h in range(HEADS):
                    dve.wait_ge(score_done, HEADS * l + h + 1)
                    dve.wait_ge(exp_ready, HEADS * l + h + 1)
                    dve.scalar_tensor_tensor(out=expo[:, h, :], in0=bank[h][:, 0:SEQ + P], scalar=SCALE,
                                             in1=expo[:, h, :], op0=ALU.mult, op1=ALU.mult).then_inc(prob_ready, 1)
                dve.wait_ge(proj_act, 16 * l + 12)
                link(dve.tensor_scalar(o_sig[:, :, :], o_sig[:, :, :], 1.0, None, ALU.add))
                link(dve.reciprocal(o_sig[:, :, :], o_sig[:, :, :]))
                dve.wait_ge(expm_ready, l + 1)
                for h in range(HEADS):
                    dve.wait_ge(pv_done, HEADS * l + h + 1)
                    last = dve.tensor_copy(den[:, :, h:h + 1], bank[h][:, 0:2 * DK + 2].rearrange("p (t d) -> p t d", t=T)[:, :, DK:DK + 1])
                link(last)
                link(dve.scalar_tensor_tensor(out=dmax[:, :, :], in0=den[:, :, :], scalar=-1.0, in1=den[:, :, :],
                                              op0=ALU.mult, op1=ALU.max))
                link(dve.tensor_tensor(dmax[:, :, :], dmax[:, :, :], exp_neg_m[:, :, :], ALU.max))
                link(dve.reciprocal(dmax[:, :, :], dmax[:, :, :]))
                for h in range(HEADS):
                    for t in range(T):
                        last = dve.tensor_scalar(hb[:, t, h * DK:(h + 1) * DK], bank[h][:, t * (DK + 1):t * (DK + 1) + DK],
                                                 dmax[:, t, h:h + 1], None, ALU.mult)
                link(last)
                for t in range(T):
                    for h in range(HEADS):
                        last = dve.bn_stats(stats_h[:, t * HEADS + h, :], hb[:, t, h * DK:(h + 1) * DK])
                link(last)
                for i in range(T * HEADS):
                    last = dve.bn_aggr(mv_h[:, i, :], stats_h[:, i, :])
                link(last)
                dve.tensor_scalar(var[:, :], mv_h[:, :, 1], EPS, None, ALU.add).then_inc(hvar_ready, 1)
                for q in range(CH):
                    dve.wait_ge(proj_done, NBLK * l + 17 + q)
                    dve.wait_ge(proj_act, 16 * l + 13 + q)
                    dve.tensor_tensor(zT[:, q, 2:2 + SEQ], ccT[:, q, :], bank[4 + q][:, 0:SEQ], ALU.mult).then_inc(proj_dve, 1)
                newton(T * HEADS, hrs_ready, l + 1)
                for t in range(T):
                    for h in range(HEADS):
                        i = t * HEADS + h
                        last = dve.tensor_scalar(hb[:, t, h * DK:(h + 1) * DK], hb[:, t, h * DK:(h + 1) * DK],
                                                 mv_h[:, i, 0:1], rstd[:, i:i + 1], ALU.subtract, ALU.mult)
                link(last)
                dve.wait_ge(rows_landed, 16 * 7 * l + 16 * 7)
                link(dve.tensor_tensor(hb[:, :, :], hb[:, :, :], mh_w[:, :].unsqueeze(1).to_broadcast([P, T, WM]), ALU.mult))
                dve.tensor_tensor(hb[:, :, :], hb[:, :, :], o_sig[:, :, :], ALU.mult).then_inc(h_ready, 1)
                for q in range(CH):
                    tap = lambda k: w_conv_col[:, l, k * CH + q:k * CH + q + 1]
                    dve.wait_ge(proj_dve, 8 * l + q + 1)
                    link(dve.tensor_scalar(convT[:, :], zT[:, q, 0:SEQ], tap(0), None, ALU.mult))
                    for k in (1, 2):
                        link(dve.scalar_tensor_tensor(out=convT[:, :], in0=zT[:, q, k:k + SEQ], scalar=tap(k),
                                                      in1=convT[:, :], op0=ALU.mult, op1=ALU.add))
                    dve.wait_ge(proj_done, NBLK * l + 21 + q)
                    dve.tensor_tensor(mixT[:, CH + q, :], convT[:, :], bank[4 + q][:, 0:SEQ], ALU.mult).then_inc(proj_dve, 1)
                    dve.wait_ge(proj_dve, 8 * l + CH + q + 1)
                gate_rows(l, 0, 4)
                dve.wait_ge(gate_row_ready, 4 * l + 2)
                residual_norm(l, 0, between=lambda: shift_scale(l))
                modulate(l, 1)

                dve.wait_ge(logT_done, l + 1)
                dve.tensor_scalar(logT[:, :], bank[6][0:G + EXPERTS, 0:SEQ], b_route_col[:, l:l + 1], None,
                                  ALU.add).then_inc(logT_copied, 1)
                dve.wait_ge(logit_done, l + 1)
                link(dve.tensor_copy(logit[:, :, :], bank[6][:, 0:64].rearrange("p (t c) -> p t c", t=T)[:, :, 0:G + EXPERTS]))
                gl = logit[:, :, 0:G]
                el = logit[:, :, G:G + EXPERTS].rearrange("p t (g e) -> p t g e", g=G)
                link(dve.tensor_reduce(gmax[:, :, :], gl, AX.X, ALU.max))
                dve.tensor_tensor(dif[:, :, 0:G], gl, gmax[:, :, :].to_broadcast([P, T, G]), ALU.subtract)
                first_of(gl, gmax[:, :, :], grp1[:, :, :])
                link(dve.tensor_tensor(ew[:, :, :, :], el, grp1[:, :, :].unsqueeze(3).to_broadcast([P, T, G, E]), ALU.mult))
                link(dve.tensor_reduce(sel[:, :, :], ew[:, :, :, :].rearrange("p t g e -> p t e g"), AX.X, ALU.add))
                link(dve.tensor_reduce(m1[:, :, :], sel[:, :, :], AX.X, ALU.max))
                first_of(sel[:, :, :], m1[:, :, :], top1[:, :, :])
                link(dve.scalar_tensor_tensor(out=sel2[:, :, :], in0=top1[:, :, :], scalar=MASKED, in1=sel[:, :, :],
                                              op0=ALU.mult, op1=ALU.add))
                link(dve.tensor_reduce(m2[:, :, :], sel2[:, :, :], AX.X, ALU.max))
                dve.tensor_tensor(dif[:, :, G:G + 1], m2[:, :, :], m1[:, :, :], ALU.subtract).then_inc(dif_ready, 1)
                first_of(sel2[:, :, :], m2[:, :, :], top2[:, :, :])
                link(dve.tensor_tensor(both[:, :, :], top1[:, :, :], top2[:, :, :], ALU.add))
                dve.tensor_tensor(mask[:, :, :].rearrange("p t (g e) -> p t g e", g=G),
                                  both[:, :, :].unsqueeze(2).to_broadcast([P, T, G, E]),
                                  grp1[:, :, :].unsqueeze(3).to_broadcast([P, T, G, E]), ALU.mult).then_inc(mask_ready, 1)
                dve.wait_ge(dexp_ready, l + 1)
                dve.tensor_reduce(wsum[:, :, 0:1], dexp[:, :, 0:G], AX.X, ALU.add)
                link(dve.tensor_scalar(wsum[:, :, 1:2], dexp[:, :, G:G + 1], 1.0, None, ALU.add))
                link(dve.tensor_tensor(wsum[:, :, 0:1], wsum[:, :, 0:1], wsum[:, :, 1:2], ALU.mult))
                link(dve.reciprocal(wsum[:, :, 0:1], wsum[:, :, 0:1]))
                link(dve.tensor_tensor(wboth[:, :, :], top2[:, :, :], dexp[:, :, G:G + 1].to_broadcast([P, T, E]), ALU.mult))
                link(dve.tensor_tensor(wboth[:, :, :], wboth[:, :, :], top1[:, :, :], ALU.add))
                link(dve.tensor_tensor(wboth[:, :, :], wboth[:, :, :], wsum[:, :, 0:1].to_broadcast([P, T, E]), ALU.mult))
                link(dve.tensor_tensor(comb[:, :, :].rearrange("p t (g e) -> p t g e", g=G),
                                       wboth[:, :, :].unsqueeze(2).to_broadcast([P, T, G, E]),
                                       grp1[:, :, :].unsqueeze(3).to_broadcast([P, T, G, E]), ALU.mult))
                dve.wait_ge(pos_done, l + 1)
                link(dve.scalar_tensor_tensor(out=pos[:, :, :], in0=bank[6][:, 0:2 * EXPERTS].rearrange("p (t e) -> p t e", t=T),
                                              scalar=1.0, in1=mask[:, :, :], op0=ALU.add, op1=ALU.mult))
                link(dve.tensor_scalar(pos[:, :, :], pos[:, :, :], -1.0, None, ALU.add))
                dve.tensor_reduce(pmax[:, :], pos[:, :, :].rearrange("p t e -> p (t e)"), AX.X, ALU.max).then_inc(pmax_ready, 1)
                build(main, 0, 0)
                gate_rows(l, 1, 10)
                build(main, 2, 1)
                dve.wait_ge(pmaxT_done, l + 1)
                link(dve.tensor_reduce(pall[:, :], bank[4][0:1, 0:P], AX.X, ALU.max))
                dve.tensor_scalar(flag[:, l:l + 1], pall[:, :], float(CAP), None, ALU.is_ge).then_inc(flag_ready, 1)

                xg_half(main, PAIRS * l)

                def pair(p, b, more=True, final=False):
                    n = PAIRS * l + p
                    hidden(main, n)
                    if not final:
                        xg_half(main, n + 1)
                    combine_copy(main, n)
                    if more:
                        build(main, 2 * p + 4, b)
                    down_copy(main, n)

                pair(0, 0)
                with dve.Fori(0, (PAIRS - 4) // 2) as i:
                    pair(2 * i + 1, 1)
                    pair(2 * i + 2, 0)
                pair(PAIRS - 3, 1)
                pair(PAIRS - 2, 0, more=False)
                pair(PAIRS - 1, 1, more=False, final=True)
                more = dve.value_load(flag[0:1, l:l + 1])
                with dve.If(more != 0):
                    S = over[l]
                    with dve.Fori(0, ROUNDS - 1) as r:
                        dve.wait_ge(S.disp, r * PAIRS)
                        dve.tensor_scalar(pos[:, :, :], pos[:, :, :], -float(CAP), None, ALU.add).then_inc(S.added, 1)
                        dve.wait_ge(S.added, (r + 1) * (PAIRS + 1) - PAIRS)
                        dve.memset(scm[:, :, :], 0.0)
                        with dve.Fori(0, PAIRS) as p:
                            n = r * PAIRS + p
                            dve.wait_ge(S.cT, n)
                            build(S, 2 * p, 0)
                            xg_half(S, n)
                            hidden(S, n)
                            combine_copy(S, n)
                            down_copy(S, n)
                        dve.wait_ge(S.added, (r + 1) * (PAIRS + 1))
                residual_norm(l, 1)


_INS = ['x', 'c', 'w_ada', 'b_ada', 'w_in', 'b_gates', 'mh_norm_w', 'w_conv', 'w_out', 'ln1_g', 'ln1_b',
        'w_grp', 'b_grp', 'w_router', 'b_router', 'w_gate', 'w_up', 'w_down', 'ln2_g', 'ln2_b']


def kernel(**inputs):
    import numpy as _np
    import concourse.bacc as _bacc
    from concourse import mybir as _mybir
    from concourse.bass_utils import run_bass_kernel_spmd as _run

    nc = _bacc.Bacc("TRN2", target_bir_lowering=False, num_devices=1)
    arrays, args = {}, []
    for name in _INS:
        a = _np.ascontiguousarray(inputs[name])
        arrays[f"in_{name}_dram"] = a
        args.append(nc.dram_tensor(f"in_{name}_dram", a.shape, _mybir.dt.from_np(a.dtype), kind="ExternalInput").ap())
    args.append(nc.dram_tensor("out_dram", arrays["in_x_dram"].shape, _mybir.dt.float32, kind="ExternalOutput").ap())
    trunk_kernel(nc, *args)
    r = _run(nc, [arrays], core_ids=[0])
    return r.results[0]["out_dram"]
```

```python
from contextlib import ExitStack

import concourse.bass as bass
from concourse import mybir

ACT = mybir.ActivationFunctionType
ALU = mybir.AluOpType
AX = mybir.AxisListType
F32 = mybir.dt.float32
BF16 = mybir.dt.bfloat16
I32 = mybir.dt.int32

P = 128
HEADS = 4
EPS = 1e-5
CAP = 64
MASKED = -1e30


def trunk_kernel(nc, x, c, w_ada, b_ada, w_in, b_gates, mh_norm_w, w_conv, w_out, ln1_g, ln1_b,
                 w_grp, b_grp, w_router, b_router, w_gate, w_up, w_down, ln2_g, ln2_b, out):
    _, SEQ, D = x.shape
    DEPTH = w_in.shape[0]
    G, E, _, F = w_gate.shape[1:]
    T = SEQ // P
    KC = D // P
    FC = F // P
    DK = D // 8
    WM = HEADS * DK
    CH = WM // P
    EXPERTS = G * E
    PAIRS = EXPERTS // 2
    ROUNDS = SEQ // CAP
    NMOD = 6 * D // P
    ALPHA = float((2 * DEPTH) ** 0.25)
    SCALE = float(DK) ** -0.5
    assert T == 2 and DK == P and WM == 512 and 2 * CAP == P and CH == HEADS and F == 512

    RING = 6
    COLS = 512
    ADA1, PROJ, ADA2, WOUT, ADA3, MOE = 0, 4, 11, 15, 17, 21
    UNITS = MOE + 6 * PAIRS
    NBLK = 24
    COL_GATES = 4 * WM
    PROJ_COL = [0, WM, 2 * WM, 3 * WM, COL_GATES + 8 + WM, COL_GATES + 8 + 2 * WM, COL_GATES + 8]
    ADA_UNIT = [ADA1 + i for i in range(4)] + [ADA2 + i for i in range(4)] + [ADA3 + i for i in range(4)]
    ADA_COL = [COLS * i for i in (0, 1, 2, 3, 6, 7, 4, 5, 8, 9, 10, 11)]
    GATE1, GATE2 = 6, 10

    ctx = ExitStack()
    with ctx:
        def sb(name, shape, dt=F32):
            return ctx.enter_context(nc.sbuf_tensor(name, shape, dt))

        def sem(name):
            return ctx.enter_context(nc.semaphore(name))

        bank = [ctx.enter_context(nc.psum_tensor(f"bank{i}", [P, COLS], F32)) for i in range(8)]

        ring = [sb(f"ring{i}", [P, KC, COLS]) for i in range(RING)]
        w_gates_sb = sb("w_gates_sb", [P, DEPTH, KC, 8])
        w_route_sb = sb("w_route_sb", [P, DEPTH, KC, G + EXPERTS])
        ident = sb("ident", [P, P])
        causal = sb("causal", [P, 3 * P])
        before = sb("before", [P, P])
        ones = sb("ones", [P, P])
        partials = sb("partials", [P, P])
        pick_i = sb("pick_i", [8, HEADS])
        pick_f = sb("pick_f", [8, HEADS])
        pick_negf = sb("pick_negf", [8, HEADS])
        head_row = sb("head_row", [HEADS, HEADS, P])
        slots = sb("slots", [P, CAP])
        prefer = sb("prefer", [P, G])
        zeros = sb("zeros", [P, COLS], BF16)
        b_gates_col = sb("b_gates_col", [8, DEPTH])
        b_route_col = sb("b_route_col", [G + EXPERTS, DEPTH])
        b_ada_col = sb("b_ada_col", [P, DEPTH, NMOD])
        w_conv_col = sb("w_conv_col", [P, DEPTH, 3 * CH])
        cond = sb("cond", [P, KC, 32])
        mh_w = sb("mh_w", [P, WM])
        ln_g = sb("ln_g", [P, 2, D])
        ln_b = sb("ln_b", [P, 2, D])
        gate_row = sb("gate_row", [P, 2, D])
        mod = sb("mod", [P, 4, KC])
        part = sb("part", [P, 2, COLS])
        X = sb("X", [P, T, D])
        uT = sb("uT", [P, KC, SEQ])
        qT = sb("qT", [P, HEADS, SEQ])
        kT = sb("kT", [P, HEADS, SEQ])
        v_ext = sb("v_ext", [P, T, HEADS, DK + 1])
        o_sig = sb("o_sig", [P, T, WM])
        ccT = sb("ccT", [P, CH, SEQ])
        zT = sb("zT", [P, CH, 2 + SEQ])
        convT = sb("convT", [P, SEQ])
        mixT = sb("mixT", [P, KC, SEQ])
        gate_pre, gate_neg, gate_ln = mixT[0:8, 0, :], mixT[0:8, 1, :], mixT[0:8, 2, :]
        a_row, neg_g, neg_m = mixT[0:HEADS, 3, :], mixT[0:HEADS, 4, :], mixT[0:HEADS, 5, :]
        hb = sb("hb", [P, T, WM])
        expo = sb("expo", [P, HEADS, 3 * P])
        b_ada_rows = expo[0:NMOD, 0, 0:DEPTH * P].rearrange("r (l p) -> r l p", l=DEPTH)
        w_conv_rows = expo[0:3 * CH, 1, 0:DEPTH * P].rearrange("r (l p) -> r l p", l=DEPTH)
        c_rows = expo[0:KC, 2, 0:P]
        cums = [sb(f"cums{i}", [8, P + SEQ]) for i in range(2)]
        maxs = [sb(f"maxs{i}", [HEADS, P + SEQ]) for i in range(2)]
        a_col = sb("a_col", [P, T, HEADS])
        exp_neg_m = sb("exp_neg_m", [P, T, HEADS])
        den = sb("den", [P, T, HEADS])
        dmax = sb("dmax", [P, T, HEADS])
        stats_h = sb("stats_h", [P, T * HEADS, 6])
        mv_h = sb("mv_h", [P, T * HEADS, 2])
        stats = sb("stats", [P, T, 2, 6])
        mv = sb("mv", [P, T, 2])
        var = sb("var", [P, 8])
        lnv = sb("lnv", [P, 8])
        rstd = sb("rstd", [P, 8])
        nt = sb("nt", [P, 8])
        tmp = sb("tmp", [P, COLS])
        logT = sb("logT", [G + EXPERTS, SEQ])
        logit = sb("logit", [P, T, G + EXPERTS])
        gmax = sb("gmax", [P, T, 1])
        grp1 = sb("grp1", [P, T, G])
        ew = sb("ew", [P, T, G, E])
        sel = sb("sel", [P, T, E])
        sel2 = sb("sel2", [P, T, E])
        top1 = sb("top1", [P, T, E])
        top2 = sb("top2", [P, T, E])
        m1 = sb("m1", [P, T, 1])
        m2 = sb("m2", [P, T, 1])
        sc = sb("sc", [P, T, E])
        scm = sb("scm", [P, T, 1])
        dif = sb("dif", [P, T, G + 1])
        dexp = sb("dexp", [P, T, G + 1])
        wsum = sb("wsum", [P, T, 3])
        both = sb("both", [P, T, E])
        wboth = sb("wboth", [P, T, E])
        comb = sb("comb", [P, T, EXPERTS])
        mask = sb("mask", [P, T, EXPERTS])
        pos = sb("pos", [P, T, EXPERTS])
        pmax = sb("pmax", [P, 1])
        pall = sb("pall", [1, 1])
        flag = sb("flag", [1, DEPTH], I32)
        disp = [ccT[:, i, :].rearrange("p (t s) -> p t s", t=T) for i in range(2)]
        dispw = [ccT[:, 2 + i, :].rearrange("p (t s) -> p t s", t=T) for i in range(2)]
        xg = qT[:, :, :].rearrange("p h s -> p (h s)").rearrange("p (k s) -> p k s", k=KC)
        dn = kT[:, :, :].rearrange("p h s -> p (h s)")
        sg, hh = o_sig[:, 0, :], o_sig[:, 1, :]
        hhT = hb[:, 0, :].rearrange("p (f s) -> p f s", f=FC)
        combT = hb[:, 1, 0:SEQ]

        landed = [sem(f"landed{i}") for i in range(RING)]
        x_landed = sem("x_landed")
        c_landed = sem("c_landed")
        cols_landed = sem("cols_landed")
        small_landed = [sem(f"small_landed{l}") for l in range(DEPTH)]
        route_landed = sem("route_landed")
        rows_landed = sem("rows_landed")
        consts = sem("consts")
        const_step = sem("const_step")
        dve_consts = sem("dve_consts")
        cT_ready, cond_ready, cols_ready, cols_copied = sem("cT_ready"), sem("cond_ready"), sem("cols_ready"), sem("cols_copied")
        ada_sum, ada_part, ada_ext = sem("ada_sum"), sem("ada_part"), sem("ada_ext")
        mod_ready, gate_row_ready = sem("mod_ready"), sem("gate_row_ready")
        xT_ready, uT_act, uT_dve = sem("xT_ready"), sem("uT_act"), sem("uT_dve")
        gates_ready, neg_ready, ln_ready, cum_ready = sem("gates_ready"), sem("neg_ready"), sem("ln_ready"), sem("cum_ready")
        aF_ready, rows_ready, bcast_ready = sem("aF_ready"), sem("rows_ready"), sem("bcast_ready")
        expm_ready, arg_ready, exp_ready = sem("expm_ready"), sem("arg_ready"), sem("exp_ready")
        proj_done, proj_act, proj_dve = sem("proj_done"), sem("proj_act"), sem("proj_dve")
        score_done, prob_ready, pv_done = sem("score_done"), sem("prob_ready"), sem("pv_done")
        hvar_ready, hrs_ready, h_ready, hT_done, hT_copied = sem("hvar_ready"), sem("hrs_ready"), sem("h_ready"), sem("hT_done"), sem("hT_copied")
        mix_done, var_ready, rs_ready, x_ready = sem("mix_done"), sem("var_ready"), sem("rs_ready"), sem("x_ready")
        logT_done, logT_copied, logit_done = sem("logT_done"), sem("logT_copied"), sem("logit_done")
        dif_ready, dexp_ready, mask_ready, pos_done = sem("dif_ready"), sem("dexp_ready"), sem("mask_ready"), sem("pos_done")
        pmax_ready, pmaxT_done, flag_ready = sem("pmax_ready"), sem("pmaxT_done"), sem("flag_ready")
        y_done = sem("y_done")
        dve_step, act_step = sem("dve_step"), sem("act_step")
        stored = sem("stored")

        class ExpertSems:
            def __init__(self, tag):
                self.disp = sem(f"disp_built{tag}")
                self.dispw = sem(f"dispw_built{tag}")
                self.gath = sem(f"gathered{tag}")
                self.xg_act = sem(f"xg_act{tag}")
                self.xg_dve = sem(f"xg_dve{tag}")
                self.gate = sem(f"gate_done{tag}")
                self.up = sem(f"up_done{tag}")
                self.sg = sem(f"silu_ready{tag}")
                self.hh = sem(f"hidden_ready{tag}")
                self.hT = sem(f"hiddenT_done{tag}")
                self.hTc = sem(f"hiddenT_copied{tag}")
                self.cT = sem(f"combineT_done{tag}")
                self.cTc = sem(f"combineT_copied{tag}")
                self.down = sem(f"down_done{tag}")
                self.dn_act = sem(f"down_act{tag}")
                self.dn_dve = sem(f"down_dve{tag}")
                self.added = sem(f"pair_added{tag}")

        main = ExpertSems("")
        over = [ExpertSems(f"_over{l}") for l in range(DEPTH)]
        over_landed = [[sem(f"over_landed{l}_{j}") for j in range(6)] for l in range(DEPTH)]

        wg_all = w_gate.rearrange("l g e (k h p) f -> p (l g e k) h f", p=P, h=2)
        wu_all = w_up.rearrange("l g e (k h p) f -> p (l g e k) h f", p=P, h=2)
        wd_all = w_down.rearrange("l g e (k p) n -> p (l g e k) n", p=P)

        def unit_source(l, u):
            if u in ADA_UNIT:
                w, col = w_ada, ADA_COL[ADA_UNIT.index(u)]
            elif u < ADA2:
                w, col = w_in, PROJ_COL[u - PROJ]
            else:
                w, col = w_out, (u - WOUT) * COLS
            return w[l].rearrange("(k p) n -> p k n", p=P)[:, :, col:col + COLS]

        def slot(l, u):
            return (l * UNITS + u) % RING

        def arrived(eng, l, u, more=0):
            eng.wait_ge(landed[slot(l, u)], 16 * ((l * UNITS + u) // RING + 1) + 16 * more)

        def blocks_before(u):
            return [4, 8, 10, 12, 16, 20, 24][u]

        def released(eng, l, u):
            if u in ADA_UNIT:
                eng.wait_ge(ada_sum, 12 * l + ADA_UNIT.index(u) + 1)
            elif u < ADA2:
                eng.wait_ge(proj_done, NBLK * l + blocks_before(u - PROJ))
            elif u < MOE:
                eng.wait_ge(mix_done, 4 * l + 2 * (u - WOUT) + 2)
            else:
                pair, j = divmod(u - MOE, 6)
                expert_released(eng, PAIRS * l + pair, j)

        def expert_released(eng, n, j):
            eng.wait_ge((main.gate, main.up, main.down)[j // 2], 2 * n + j % 2 + 1)

        def expert_dma(eng, l, p, j, s, signal):
            first = (l * EXPERTS + 2 * p) * 4
            rows = slice(first, first + 8) if isinstance(first, int) else bass.ds(first, 8)
            h = j % 2
            src = (wg_all, wu_all)[j // 2][:, rows, h, :] if j < 4 else wd_all[:, rows, h * COLS:(h + 1) * COLS]
            eng.dma_start(ring[s][:, :, :], src).then_inc(signal, 16)

        def load_gates(eng, l):
            eng.dma_start(b_gates_col[:, l:l + 1], b_gates[l].rearrange("(k a) -> k a", a=1)).then_inc(small_landed[l], 16)
            eng.dma_start(w_gates_sb[:, l, :, :], w_in[l].rearrange("(k p) n -> p k n", p=P)[:, :, COL_GATES:COL_GATES + 8]).then_inc(small_landed[l], 16)

        block = ctx.enter_context(nc.Block())

        @block.sync
        def _(sp):
            sp.dma_start(c_rows, c.rearrange("a (k p) -> (a k) p", p=P)).then_inc(c_landed, 16)
            for l in range(DEPTH):
                sp.dma_start(b_ada_rows[:, l, :], b_ada[l].rearrange("(k p) -> k p", p=P)).then_inc(cols_landed, 16)
                sp.dma_start(w_conv_rows[:, l, :], w_conv[l].rearrange("k (c p) -> (k c) p", p=P)).then_inc(cols_landed, 16)
            for l in range(DEPTH):
                for u in range(MOE):
                    if l == 0 and u == PROJ:
                        for t in range(T):
                            sp.dma_start(X[:, t, :], x[0, t * P:(t + 1) * P, :]).then_inc(x_landed, 16)
                    if l * UNITS + u >= RING:
                        prev = (l, u - RING) if u >= RING else (l - 1, UNITS + u - RING)
                        released(sp, *prev)
                    sp.dma_start(ring[slot(l, u)][:, :, :], unit_source(l, u)).then_inc(landed[slot(l, u)], 16)
                for j in range(6):
                    released(sp, l, MOE + j - RING)
                    expert_dma(sp, l, 0, j, slot(l, MOE + j), landed[slot(l, MOE + j)])
                with sp.Fori(1, PAIRS) as p:
                    for j in range(6):
                        expert_released(sp, PAIRS * l + p - 1, j)
                        expert_dma(sp, l, p, j, slot(l, MOE + j), landed[slot(l, MOE + j)])
                sp.wait_ge(flag_ready, l + 1)
                more = sp.value_load(flag[0:1, l:l + 1])
                with sp.If(more != 0):
                    sp.wait_ge(main.down, 2 * PAIRS * (l + 1))
                    with sp.Fori(0, ROUNDS - 1) as r:
                        with sp.Fori(0, PAIRS) as p:
                            for j in range(6):
                                sp.wait_ge(over[l].down, 2 * (r * PAIRS + p))
                                expert_dma(sp, l, p, j, slot(l, MOE + j), over_landed[l][j])
                    sp.wait_ge(over[l].down, 2 * (ROUNDS - 1) * PAIRS)
            for t in range(T):
                sp.wait_ge(x_ready, 2 * T * (DEPTH - 1) + T + t + 1)
                sp.dma_start(out[0, t * P:(t + 1) * P, :], X[:, t, :]).then_inc(stored, 16)
            sp.wait_ge(stored, 16 * T)

        @block.gpsimd
        def _(pool):
            def select(t, pattern, base, cm, op, fill):
                return pool.affine_select(out=t, in_=t, compare_op=op, fill=fill, base=base,
                                          pattern=pattern, channel_multiplier=cm)

            def load_rows(l, which):
                g, b = ((ln1_g, ln1_b), (ln2_g, ln2_b))[which]
                gt = (2, 5)[which]
                pool.dma_start(gate_row[:, which, :], b_ada[l, gt * D:(gt + 1) * D].partition_broadcast(P)).then_inc(rows_landed, 16)
                pool.dma_start(ln_g[:, which, :], g[l].partition_broadcast(P)).then_inc(rows_landed, 16)
                pool.dma_start(ln_b[:, which, :], b[l].partition_broadcast(P)).then_inc(rows_landed, 16)
                if which == 0:
                    pool.dma_start(mh_w[:, :], mh_norm_w[l].partition_broadcast(P)).then_inc(rows_landed, 16)

            pool.memset(ident[:, :], 0.0).then_inc(const_step, 1)
            pool.memset(partials[:, :], 0.0).then_inc(const_step, 1)
            pool.memset(causal[:, :], 0.0).then_inc(const_step, 1)
            pool.memset(before[:, :], 1.0).then_inc(const_step, 1)
            pool.memset(ones[:, :], 1.0).then_inc(const_step, 1)
            pool.memset(pick_i[:, :], 0.0).then_inc(const_step, 1)
            pool.memset(pick_f[:, :], 0.0).then_inc(const_step, 1)
            pool.memset(pick_negf[:, :], 0.0).then_inc(const_step, 1)
            pool.memset(head_row[:, :, :], 0.0).then_inc(const_step, 1)
            pool.wait_ge(const_step, 9)
            select(ident[:, :], [[-1, P]], 0, 1, ALU.not_equal, 1.0).then_inc(const_step, 1)
            for r in range(4):
                pool.wait_ge(const_step, 10 + r)
                pool.memset(partials[32 * r:32 * r + 1, :], 1.0).then_inc(const_step, 1)
            pool.wait_ge(const_step, 14)
            select(causal[:, 0:SEQ], [[1, SEQ]], 0, -1, ALU.is_ge, MASKED).then_inc(const_step, 1)
            select(causal[:, SEQ:SEQ + P], [[1, P]], 0, -1, ALU.is_ge, MASKED).then_inc(const_step, 1)
            select(before[:, :], [[1, P]], 0, -1, ALU.is_gt, 0.0).then_inc(const_step, 1)
            select(pick_i[:, :], [[-1, HEADS]], 0, 1, ALU.not_equal, 1.0).then_inc(const_step, 1)
            select(pick_f[:, :], [[-1, HEADS]], -HEADS, 1, ALU.not_equal, 1.0).then_inc(const_step, 1)
            select(pick_negf[:, :], [[-1, HEADS]], -HEADS, 1, ALU.not_equal, -1.0).then_inc(const_step, 1)
            select(head_row[:, :, :], [[-1, HEADS], [0, P]], 0, 1, ALU.not_equal, 1.0).then_inc(const_step, 1)
            pool.iota(slots[:, :], pattern=[[1, CAP]], base=0, channel_multiplier=0,
                      allow_small_or_imprecise_dtypes=True).then_inc(const_step, 1)
            pool.iota(prefer[:, :], pattern=[[-1, G]], base=G, channel_multiplier=0,
                      allow_small_or_imprecise_dtypes=True).then_inc(const_step, 1)
            pool.wait_ge(const_step, 23)
            pool.memset(tmp[:, 0:1], 0.0).then_inc(consts, 1)

            for l in range(DEPTH):
                if l:
                    pool.wait_ge(x_ready, 2 * T * l)
                arrived(pool, l, PROJ + 1)
                load_rows(l, 0)
                load_rows(l, 1)

        @block.tensor
        def _(pe):
            def ada_unit(l, i):
                n = 12 * l + i
                if i >= 2:
                    pe.wait_ge(ada_part, n - 1)
                arrived(pe, l, ADA_UNIT[i])
                w = ring[slot(l, ADA_UNIT[i])]
                for kc in range(KC):
                    g = kc % 4
                    last = pe.matmul(bank[4 + i % 2][32 * g:32 * g + 32, :], cond[:, kc, :], w[:, kc, :],
                                     start=(kc < 4), stop=(kc >= 4), tile_position=(0, 32 * g))
                last.then_inc(ada_sum, 1)

            def ada_extract(l, i):
                pe.wait_ge(ada_part, 12 * l + i + 1)
                if i // 2 * 2 in (GATE1, GATE2):
                    last = pe.matmul(bank[4 + i % 2][:, :], partials[:, :], part[:, i % 2, :], start=True, stop=True)
                else:
                    for q in range(4):
                        last = pe.matmul(bank[6][:, 4 * i + q:4 * i + q + 1], part[:, i % 2, q * P:(q + 1) * P],
                                         partials[:, 0:1], start=True, stop=True)
                last.then_inc(ada_ext, 1)

            def ada_units(l, first, n):
                for i in range(first, first + n):
                    ada_unit(l, i)
                    if i > first:
                        ada_extract(l, i - 1)
                ada_extract(l, first + n - 1)

            def transpose_x(ready, value, step):
                for t in range(T):
                    pe.wait_ge(ready, value + t * step)
                    for kc in range(KC):
                        o = (kc % 2) * SEQ + t * P
                        last = pe.transpose(bank[kc // 2][:, o:o + P], X[:, t, kc * P:(kc + 1) * P], ident[:, :])
                        if kc % 2 and t == T - 1:
                            last.then_inc(xT_ready, 1)

            def wait_block(l, b):
                if b >= 4:
                    if b - 4 < 16:
                        pe.wait_ge(proj_act, 16 * l + b - 3)
                    else:
                        pe.wait_ge(proj_dve, 8 * l + b - 19)

            def proj_channels(l, u, b0):
                arrived(pe, l, PROJ + u)
                w = ring[slot(l, PROJ + u)]
                for q in range(4):
                    wait_block(l, b0 + q)
                    for kc in range(KC):
                        last = pe.matmul(bank[4 + (b0 + q) % 4][:, 0:SEQ], w[:, kc, q * P:(q + 1) * P],
                                         uT[:, kc, :], start=(kc == 0), stop=(kc == KC - 1))
                    last.then_inc(proj_done, 1)

            def proj_tokens(l, u, b0):
                arrived(pe, l, PROJ + u)
                w = ring[slot(l, PROJ + u)]
                for t in range(T):
                    wait_block(l, b0 + t)
                    for kc in range(KC):
                        last = pe.matmul(bank[4 + (b0 + t) % 4][:, :], uT[:, kc, t * P:(t + 1) * P],
                                         w[:, kc, :], start=(kc == 0), stop=(kc == KC - 1))
                    last.then_inc(proj_done, 1)

            def gather(S, n, b):
                pe.wait_ge(S.disp, n + 1)
                for kc in range(KC):
                    for t in range(T):
                        last = pe.matmul(bank[6 + kc // 4][:, (kc % 4) * P:(kc % 4 + 1) * P],
                                         X[:, t, kc * P:(kc + 1) * P], disp[b][:, t, :],
                                         start=(t == 0), stop=(t == T - 1))
                    if kc % 4 == 3:
                        last.then_inc(S.gath, 1)

            def gate_up(bk, s, here, done):
                for h in range(2):
                    here(h)
                    for k in range(4):
                        for j in range(2):
                            last = pe.matmul(bank[bk][CAP * j:CAP * (j + 1), :], xg[:, 2 * k + h, CAP * j:CAP * (j + 1)],
                                             ring[s[h]][:, 4 * j + k, :], start=(h == 0 and k == 0),
                                             stop=(h == 1 and k == 3), tile_position=(0, CAP * j))
                    last.then_inc(done, 1)

            def hidden_T(S, n):
                pe.wait_ge(S.hh, n + 1)
                for f in range(FC):
                    last = pe.transpose(bank[6][:, f * P:(f + 1) * P], hh[:, f * P:(f + 1) * P], ident[:, :])
                last.then_inc(S.hT, 1)

            def combine_T(S, n, b):
                pe.wait_ge(S.dispw, n + 1)
                for t in range(T):
                    last = pe.transpose(bank[7][:, t * P:(t + 1) * P], dispw[b][:, t, :], ident[:, :])
                last.then_inc(S.cT, 1)

            def down(S, n, s, here):
                for half in range(2):
                    if half == 0:
                        pe.wait_ge(S.hTc, n + 1)
                    else:
                        pe.wait_ge(S.cTc, n + 1)
                    here(half)
                    for f in range(FC):
                        for j in range(2):
                            last = pe.matmul(bank[6 + half][CAP * j:CAP * (j + 1), :], hhT[:, f, CAP * j:CAP * (j + 1)],
                                             ring[s[half]][:, 4 * j + f, :],
                                             start=(f == 0), stop=(f == FC - 1), tile_position=(0, CAP * j))
                    last.then_inc(S.down, 1)

            def combine(S, n):
                pe.wait_ge(S.cTc, n + 1)
                for half in range(2):
                    pe.wait_ge((S.dn_act, S.dn_dve)[half], n + 1)
                    for t in range(T):
                        last = pe.matmul(bank[2 * t + half][:, :], combT[:, t * P:(t + 1) * P],
                                         dn[:, half * COLS:(half + 1) * COLS], start=False, stop=False,
                                         skip_group_check=True)
                last.then_inc(S.added, 1)

            def pair(l, p, b, first=False, final=False):
                n = PAIRS * l + p
                turn = p
                s = [slot(l, MOE + j) for j in range(6)]
                pe.wait_ge(main.xg_act, n + 1)
                pe.wait_ge(main.xg_dve, n + 1)
                gate_up(4, s[0:2], lambda i: arrived(pe, l, MOE + i, turn), main.gate)
                if first:
                    pe.wait_ge(flag_ready, l + 1)
                else:
                    combine(main, n - 1)
                gate_up(5, s[2:4], lambda i: arrived(pe, l, MOE + 2 + i, turn), main.up)
                if not final:
                    gather(main, n + 1, 1 - b)
                    pe.wait_ge(main.xg_act, n + 2)
                hidden_T(main, n)
                if not final:
                    pe.wait_ge(main.xg_dve, n + 2)
                combine_T(main, n, b)
                down(main, n, s[4:6], lambda i: arrived(pe, l, MOE + 4 + i, turn))

            pe.wait_ge(consts, 1)
            pe.wait_ge(c_landed, 16)
            pe.transpose(bank[6][:, 256:256 + KC], c_rows, ident[0:KC, 0:KC]).then_inc(cT_ready, 1)
            pe.wait_ge(cols_landed, 16 * 2 * DEPTH)
            for i in range(DEPTH):
                pe.transpose(bank[7][:, 64 * i:64 * i + NMOD], b_ada_rows[:, i, :], ident[0:NMOD, 0:NMOD])
                last = pe.transpose(bank[7][:, 128 + 16 * i:128 + 16 * i + 3 * CH], w_conv_rows[:, i, :],
                                    ident[0:3 * CH, 0:3 * CH])
            last.then_inc(cols_ready, 1)
            pe.wait_ge(cond_ready, 1)

            for l in range(DEPTH):
                ada_units(l, 0, 4)
                if l == 0:
                    transpose_x(x_landed, 16 * T, 0)
                else:
                    transpose_x(x_ready, 2 * T * l - T + 1, 1)
                pe.wait_ge(uT_act, 8 * l + 4)
                pe.wait_ge(uT_dve, 8 * l + 4)
                pe.wait_ge(small_landed[l], 16 * 2)
                for kc in range(KC):
                    last = pe.matmul(bank[3][0:8, 0:SEQ], w_gates_sb[:, l, kc, :], uT[:, kc, :],
                                     start=(kc == 0), stop=(kc == KC - 1))
                last.then_inc(gates_ready, 1)
                proj_channels(l, 0, 0)
                pe.wait_ge(cum_ready, l + 1)
                pe.matmul(bank[2][0:HEADS, 0:SEQ], pick_i[:, :], gate_pre, start=True, stop=False)
                pe.matmul(bank[2][0:HEADS, 0:SEQ], pick_negf[:, :], cums[0][:, P:P + SEQ], start=False, stop=True)
                pe.matmul(bank[2][0:HEADS, SEQ:2 * SEQ], pick_f[:, :], cums[0][:, P:P + SEQ],
                          start=True, stop=True).then_inc(aF_ready, 1)
                proj_channels(l, 1, 4)
                pe.wait_ge(rows_ready, l + 1)
                for t in range(T):
                    pe.transpose(bank[3][:, 8 * t:8 * t + HEADS], a_row[:, t * P:(t + 1) * P], ident[0:HEADS, 0:HEADS])
                    pe.transpose(bank[2][:, 8 * t:8 * t + HEADS], neg_m[:, t * P:(t + 1) * P], ident[0:HEADS, 0:HEADS])
                for h in range(HEADS):
                    last = pe.matmul(bank[h // 2][:, (h % 2) * SEQ:(h % 2 + 1) * SEQ], head_row[:, h, :],
                                     neg_g, start=True, stop=True)
                last.then_inc(bcast_ready, 1)
                proj_tokens(l, 2, 8)
                pe.wait_ge(proj_act, 16 * l + 8)
                pe.wait_ge(arg_ready, HEADS * (l + 1))
                pe.wait_ge(expm_ready, l + 1)
                for h in range(HEADS):
                    pe.matmul(bank[h][:, 0:SEQ], kT[:, h, 0:P], qT[:, h, :], start=True, stop=True)
                    pe.matmul(bank[h][:, SEQ:SEQ + P], kT[:, h, P:SEQ], qT[:, h, P:SEQ],
                              start=True, stop=True).then_inc(score_done, 1)
                proj_tokens(l, 3, 10)
                proj_channels(l, 4, 12)
                pe.wait_ge(proj_act, 16 * l + 10)
                for h in range(HEADS):
                    pe.wait_ge(prob_ready, HEADS * l + h + 1)
                    pe.matmul(bank[h][:, 0:DK + 1], expo[:, h, 0:P], v_ext[:, 0, h, :], start=True, stop=True)
                    pe.matmul(bank[h][:, DK + 1:2 * DK + 2], expo[:, h, P:SEQ], v_ext[:, 0, h, :], start=True, stop=False)
                    pe.matmul(bank[h][:, DK + 1:2 * DK + 2], expo[:, h, SEQ:SEQ + P], v_ext[:, 1, h, :],
                              start=False, stop=True).then_inc(pv_done, 1)
                proj_channels(l, 5, 16)
                proj_channels(l, 6, 20)
                pe.wait_ge(proj_dve, 8 * l + 8)
                ada_units(l, 4, 4)
                pe.wait_ge(h_ready, l + 1)
                pe.wait_ge(gate_row_ready, 4 * l + 2)
                for h in range(HEADS):
                    for t in range(T):
                        o = (h % 2) * SEQ + t * P
                        last = pe.transpose(bank[4 + h // 2][:, o:o + P], hb[:, t, h * DK:(h + 1) * DK], ident[:, :])
                    if h % 2:
                        last.then_inc(hT_done, 1)
                pe.wait_ge(hT_copied, 2 * (l + 1))
                for half in range(2):
                    arrived(pe, l, WOUT + half)
                    w = ring[slot(l, WOUT + half)]
                    for t in range(T):
                        for kc in range(KC):
                            last = pe.matmul(bank[2 * t + half][:, :], mixT[:, kc, t * P:(t + 1) * P], w[:, kc, :],
                                             start=(kc == 0), stop=(kc == KC - 1))
                        last.then_inc(mix_done, 1)
                ada_units(l, 8, 2)
                transpose_x(x_ready, 2 * T * l + 1, 1)
                pe.wait_ge(uT_act, 8 * l + 8)
                pe.wait_ge(uT_dve, 8 * l + 8)
                pe.wait_ge(route_landed, 16 * 4 * DEPTH)
                for kc in range(KC):
                    last = pe.matmul(bank[6][0:G + EXPERTS, 0:SEQ], w_route_sb[:, l, kc, :], uT[:, kc, :],
                                     start=(kc == 0), stop=(kc == KC - 1))
                last.then_inc(logT_done, 1)
                for b in range(4):
                    pe.matmul(bank[b][:, :], zeros[:, 0:P], zeros[:, :], start=True, stop=False, skip_group_check=True)
                pe.wait_ge(logT_copied, l + 1)
                for t in range(T):
                    last = pe.transpose(bank[6][:, 32 * t:32 * t + G + EXPERTS], logT[:, t * P:(t + 1) * P],
                                        ident[0:G + EXPERTS, 0:G + EXPERTS])
                last.then_inc(logit_done, 1)
                ada_unit(l, GATE2)
                ada_unit(l, GATE2 + 1)
                pe.wait_ge(mask_ready, l + 1)
                pe.matmul(bank[6][:, 0:EXPERTS], before[:, :], mask[:, 0, :], start=True, stop=True)
                pe.matmul(bank[6][:, EXPERTS:2 * EXPERTS], ones[:, :], mask[:, 0, :], start=True, stop=False)
                pe.matmul(bank[6][:, EXPERTS:2 * EXPERTS], before[:, :], mask[:, 1, :],
                          start=False, stop=True).then_inc(pos_done, 1)
                ada_extract(l, GATE2)
                ada_extract(l, GATE2 + 1)

                gather(main, PAIRS * l, 0)
                pe.wait_ge(gate_row_ready, 4 * l + 4)
                pe.wait_ge(pmax_ready, l + 1)
                pe.transpose(bank[5][0:1, 0:P], pmax[:, :], ident[:, :]).then_inc(pmaxT_done, 1)
                pair(l, 0, 0, first=True)
                with pe.Fori(0, (PAIRS - 2) // 2) as i:
                    pair(l, 2 * i + 1, 1)
                    pair(l, 2 * i + 2, 0)
                pair(l, PAIRS - 1, 1, final=True)
                combine(main, PAIRS * (l + 1) - 1)
                more = pe.value_load(flag[0:1, l:l + 1])
                with pe.If(more != 0):
                    S = over[l]
                    s = [slot(l, MOE + j) for j in range(6)]
                    with pe.Fori(0, ROUNDS - 1) as r:
                        with pe.Fori(0, PAIRS) as p:
                            n = r * PAIRS + p
                            gather(S, n, 0)
                            pe.wait_ge(S.xg_act, n + 1)
                            pe.wait_ge(S.xg_dve, n + 1)
                            here = lambda j: pe.wait_ge(over_landed[l][j], 16 * n + 16)
                            gate_up(4, s[0:2], lambda i: here(i), S.gate)
                            gate_up(5, s[2:4], lambda i: here(2 + i), S.up)
                            hidden_T(S, n)
                            combine_T(S, n, 0)
                            down(S, n, s[4:6], lambda i: here(4 + i))
                            combine(S, n)
                pe.matmul(bank[0][:, :], zeros[:, 0:P], zeros[:, :], start=False, stop=True,
                          skip_group_check=True).then_inc(y_done, 1)

        @block.scalar
        def _(act):
            steps = [0]

            def link(ins):
                steps[0] += 1
                ins.then_inc(act_step, 1)
                act.wait_ge(act_step, steps[0])

            def ada_copies(l, first, n):
                for i in range(first, first + n):
                    act.wait_ge(ada_sum, 12 * l + i + 1)
                    if 12 * l + i >= 2:
                        act.wait_ge(ada_ext, 12 * l + i - 1)
                    act.activation(part[:, i % 2, :], bank[4 + i % 2][:, :], ACT.Copy).then_inc(ada_part, 1)

            def modulate(l, which):
                for kc in (2, 3, 6, 7):
                    act.wait_ge(xT_ready, 8 * l + 4 * which + kc // 2 + 1)
                    act.activation(uT[:, kc, :], bank[kc // 2][:, (kc % 2) * SEQ:(kc % 2 + 1) * SEQ], ACT.Identity,
                                   bias=mod[:, 2 * which, kc:kc + 1], scale=mod[:, 2 * which + 1, kc:kc + 1]).then_inc(uT_act, 1)

            def rsqrt(first, n, ready, value, done):
                act.wait_ge(ready, value)
                link(act.activation(lnv[:, first:first + n], var[:, first:first + n], ACT.Ln))
                act.activation(rstd[:, first:first + n], lnv[:, first:first + n], ACT.Exp, scale=-0.5).then_inc(done, 1)

            def ln_rsqrt(l, which, t):
                rsqrt(t, 1, var_ready, T * (2 * l + which) + t + 1, rs_ready)

            def xg_half(S, n):
                act.wait_ge(S.gath, 2 * n + 1)
                for kc in range(4):
                    last = act.activation(xg[:, kc, :], bank[6][:, kc * P:(kc + 1) * P], ACT.Identity,
                                          bias=mod[:, 2, kc:kc + 1], scale=mod[:, 3, kc:kc + 1])
                last.then_inc(S.xg_act, 1)

            def silu(S, n):
                act.wait_ge(S.gate, 2 * n + 2)
                act.wait_ge(S.hh, n)
                act.activation(sg, bank[4][:, :], ACT.Silu).then_inc(S.sg, 1)

            def copies(S, n):
                act.wait_ge(S.hT, n + 1)
                act.activation(hb[:, 0, :], bank[6][:, :], ACT.Copy).then_inc(S.hTc, 1)
                act.wait_ge(S.down, 2 * n + 1)
                act.activation(dn[:, 0:COLS], bank[6][:, :], ACT.Copy).then_inc(S.dn_act, 1)

            load_gates(act, 0)
            act.wait_ge(cT_ready, 1)
            for kc in range(KC):
                last = act.activation(cond[:, kc, :], bank[6][:, 256 + kc:257 + kc].to_broadcast([P, 32]), ACT.Silu)
            last.then_inc(cond_ready, 1)

            for l in range(DEPTH):
                done = T if l else 0
                ada_copies(l, done, 4 - done)
                if l == 0:
                    for i in range(1, DEPTH):
                        load_gates(act, i)
                    for i in range(DEPTH):
                        act.dma_start(b_route_col[0:G, i:i + 1], b_grp[i].rearrange("(k a) -> k a", a=1)).then_inc(route_landed, 16)
                        act.dma_start(b_route_col[G:G + EXPERTS, i:i + 1], b_router[i].rearrange("(k a) -> k a", a=1)).then_inc(route_landed, 16)
                        act.dma_start(w_route_sb[:, i, :, 0:G], w_grp[i].rearrange("(k p) n -> p k n", p=P)).then_inc(route_landed, 16)
                        act.dma_start(w_route_sb[:, i, :, G:G + EXPERTS], w_router[i].rearrange("(k p) n -> p k n", p=P)).then_inc(route_landed, 16)
                act.wait_ge(mod_ready, 2 * l + 1)
                modulate(l, 0)
                act.wait_ge(neg_ready, l + 1)
                link(act.activation(gate_ln, gate_neg, ACT.Exp))
                act.activation(gate_ln, gate_ln, ACT.Ln, bias=1.0).then_inc(ln_ready, 1)
                for b in range(8):
                    act.wait_ge(proj_done, NBLK * l + b + 1)
                    act.activation((qT, kT)[b // 4][:, b % 4, :], bank[4 + b % 4][:, 0:SEQ], ACT.Copy).then_inc(proj_act, 1)
                act.wait_ge(bcast_ready, l + 1)
                act.activation(exp_neg_m[:, :, :], bank[2][:, 0:16].rearrange("p (t c) -> p t c", t=T)[:, :, 0:HEADS],
                               ACT.Exp).then_inc(expm_ready, 1)
                for h in range(HEADS):
                    act.wait_ge(arg_ready, HEADS * l + h + 1)
                    act.activation(expo[:, h, :], expo[:, h, :], ACT.Exp).then_inc(exp_ready, 1)
                for t in range(T):
                    act.wait_ge(proj_done, NBLK * l + 9 + t)
                    if t == 0:
                        act.wait_ge(dve_consts, 1)
                    act.activation(v_ext[:, t, :, 0:DK], bank[4 + t][:, :].rearrange("p (h d) -> p h d", h=HEADS),
                                   ACT.Copy).then_inc(proj_act, 1)
                for t in range(T):
                    act.wait_ge(proj_done, NBLK * l + 11 + t)
                    act.activation(o_sig[:, t, :], bank[6 + t][:, :], ACT.Exp, scale=-1.0).then_inc(proj_act, 1)
                for q in range(CH):
                    act.wait_ge(proj_done, NBLK * l + 13 + q)
                    act.activation(ccT[:, q, :], bank[4 + q][:, 0:SEQ], ACT.Copy).then_inc(proj_act, 1)
                rsqrt(0, T * HEADS, hvar_ready, l + 1, hrs_ready)
                ada_copies(l, 4, 4)
                for b in range(2):
                    act.wait_ge(hT_done, 2 * l + b + 1)
                    act.activation(mixT[:, 2 * b:2 * b + 2, :], bank[4 + b][:, :].rearrange("p (h s) -> p h s", h=2),
                                   ACT.Copy).then_inc(hT_copied, 1)
                ln_rsqrt(l, 0, 0)
                ada_copies(l, 8, 1)
                ln_rsqrt(l, 0, 1)
                ada_copies(l, 9, 1)
                act.wait_ge(mod_ready, 2 * l + 2)
                modulate(l, 1)
                act.wait_ge(dif_ready, l + 1)
                act.activation(dexp[:, :, :], dif[:, :, :], ACT.Exp).then_inc(dexp_ready, 1)
                ada_copies(l, GATE2, 2)
                xg_half(main, PAIRS * l)

                def pair(p, final=False):
                    n = PAIRS * l + p
                    silu(main, n)
                    if not final:
                        xg_half(main, n + 1)
                    copies(main, n)

                pair(0)
                with act.Fori(0, PAIRS - 2) as p:
                    pair(p + 1)
                pair(PAIRS - 1, final=True)
                act.wait_ge(flag_ready, l + 1)
                more = act.value_load(flag[0:1, l:l + 1])
                with act.If(more != 0):
                    with act.Fori(0, ROUNDS - 1) as r:
                        with act.Fori(0, PAIRS) as p:
                            xg_half(over[l], r * PAIRS + p)
                            silu(over[l], r * PAIRS + p)
                            copies(over[l], r * PAIRS + p)
                for t in range(T):
                    if l + 1 < DEPTH:
                        ada_copies(l + 1, t, 1)
                    ln_rsqrt(l, 1, t)

        @block.vector
        def _(dve):
            steps = [0]

            def link(ins):
                steps[0] += 1
                ins.then_inc(dve_step, 1)
                dve.wait_ge(dve_step, steps[0])

            def modulate(l, which):
                for kc in (0, 1, 4, 5):
                    dve.wait_ge(xT_ready, 8 * l + 4 * which + kc // 2 + 1)
                    dve.tensor_scalar(uT[:, kc, :], bank[kc // 2][:, (kc % 2) * SEQ:(kc % 2 + 1) * SEQ],
                                      mod[:, 2 * which + 1, kc:kc + 1], mod[:, 2 * which, kc:kc + 1],
                                      ALU.mult, ALU.add).then_inc(uT_dve, 1)

            def newton(first, n, ready, value):
                dve.wait_ge(ready, value)
                link(dve.tensor_tensor(nt[:, first:first + n], rstd[:, first:first + n], rstd[:, first:first + n], ALU.mult))
                link(dve.tensor_tensor(nt[:, first:first + n], nt[:, first:first + n], var[:, first:first + n], ALU.mult))
                link(dve.tensor_scalar(nt[:, first:first + n], nt[:, first:first + n], -0.5, 1.5, ALU.mult, ALU.add))
                link(dve.tensor_tensor(rstd[:, first:first + n], rstd[:, first:first + n], nt[:, first:first + n], ALU.mult))

            def gate_rows(l, which, i0):
                for half in range(2):
                    dve.wait_ge(ada_ext, 12 * l + i0 + half + 1)
                    cols = slice(half * COLS, (half + 1) * COLS)
                    dve.scalar_tensor_tensor(out=gate_row[:, which, cols], in0=bank[4 + half][:, :], scalar=1.0,
                                             in1=gate_row[:, which, cols], op0=ALU.add, op1=ALU.add).then_inc(gate_row_ready, 1)

            def shift_scale(l):
                dve.wait_ge(ada_ext, 12 * l + 10)
                dve.tensor_tensor(mod[:, 2, :], bank[6][:, 2 * KC:3 * KC], b_ada_col[:, l, 3 * KC:4 * KC], ALU.add)
                dve.scalar_tensor_tensor(out=mod[:, 3, :], in0=bank[6][:, 4 * KC:5 * KC], scalar=1.0,
                                         in1=b_ada_col[:, l, 4 * KC:5 * KC], op0=ALU.add, op1=ALU.add).then_inc(mod_ready, 1)

            def residual_norm(l, which, between=None):
                def add(t, half):
                    if which == 0:
                        dve.wait_ge(mix_done, 4 * l + 2 * half + t + 1)
                    elif half == 0 and t == 0:
                        dve.wait_ge(y_done, l + 1)
                    cols = slice(half * COLS, (half + 1) * COLS)
                    link(dve.tensor_tensor(tmp[:, :], bank[2 * t + half][:, :], gate_row[:, which, cols], ALU.mult))
                    link(dve.scalar_tensor_tensor(out=X[:, t, cols], in0=X[:, t, cols], scalar=ALPHA,
                                                  in1=tmp[:, :], op0=ALU.mult, op1=ALU.add))
                    link(dve.bn_stats(stats[:, t, half, :], X[:, t, cols]))

                def moments(t):
                    link(dve.bn_aggr(mv[:, t, :], stats[:, t, :, :].rearrange("p a b -> p (a b)")))
                    dve.tensor_scalar(var[:, t:t + 1], mv[:, t, 1:2], EPS, None, ALU.add).then_inc(var_ready, 1)

                def centre(t):
                    link(dve.scalar_tensor_tensor(out=X[:, t, :], in0=X[:, t, :], scalar=mv[:, t, 0:1],
                                                  in1=ln_g[:, which, :], op0=ALU.subtract, op1=ALU.mult))

                def finish(t):
                    newton(t, 1, rs_ready, T * (2 * l + which) + t + 1)
                    dve.scalar_tensor_tensor(out=X[:, t, :], in0=X[:, t, :], scalar=rstd[:, t:t + 1],
                                             in1=ln_b[:, which, :], op0=ALU.mult, op1=ALU.add).then_inc(x_ready, 1)

                add(0, 0)
                if which == 0:
                    add(1, 0)
                add(0, 1)
                moments(0)
                if which == 0:
                    centre(0)
                else:
                    add(1, 0)
                add(1, 1)
                moments(1)
                if which == 1:
                    centre(0)
                finish(0)
                centre(1)
                finish(1)
                if between:
                    between()
                    dve.wait_ge(mod_ready, 2 * l + 2)

            def first_of(value, biggest, chosen):
                link(dve.tensor_tensor(sc[:, :, :], value, biggest.to_broadcast([P, T, E]), ALU.is_equal))
                link(dve.tensor_tensor(sc[:, :, :], sc[:, :, :], prefer[:, :].unsqueeze(1).to_broadcast([P, T, E]), ALU.mult))
                link(dve.tensor_reduce(scm[:, :, :], sc[:, :, :], AX.X, ALU.max))
                link(dve.tensor_tensor(chosen, sc[:, :, :], scm[:, :, :].to_broadcast([P, T, E]), ALU.is_equal))

            def halves(e0):
                for j in range(2):
                    e = e0 + j
                    yield slice(CAP * j, CAP * (j + 1)), slice(e, e + 1) if isinstance(e, int) else bass.ds(e, 1)

            def build_disp(S, e0, b):
                for half, e in halves(e0):
                    for t in range(T):
                        last = dve.tensor_scalar(disp[b][:, t, half], slots[:, :], pos[:, t, e], None, ALU.is_equal)
                last.then_inc(S.disp, 1)

            def build_dispw(S, e0, b):
                for half, e in halves(e0):
                    for t in range(T):
                        last = dve.tensor_scalar(dispw[b][:, t, half], slots[:, :], pos[:, t, e], comb[:, t, e],
                                                 ALU.is_equal, ALU.mult)
                last.then_inc(S.dispw, 1)

            def build(S, e0, b):
                build_disp(S, e0, b)
                build_dispw(S, e0, b)

            def xg_half(S, n):
                dve.wait_ge(S.gath, 2 * n + 2)
                for kc in range(4, KC):
                    last = dve.tensor_scalar(xg[:, kc, :], bank[7][:, (kc - 4) * P:(kc - 3) * P], mod[:, 3, kc:kc + 1],
                                             mod[:, 2, kc:kc + 1], ALU.mult, ALU.add)
                last.then_inc(S.xg_dve, 1)

            def hidden(S, n):
                dve.wait_ge(S.sg, n + 1)
                dve.wait_ge(S.up, 2 * n + 2)
                dve.wait_ge(S.hT, n)
                dve.tensor_tensor(hh, sg, bank[5][:, :], ALU.mult).then_inc(S.hh, 1)

            def combine_copy(S, n):
                dve.wait_ge(S.cT, n + 1)
                dve.tensor_copy(combT, bank[7][:, 0:SEQ]).then_inc(S.cTc, 1)

            def down_copy(S, n):
                dve.wait_ge(S.down, 2 * n + 2)
                dve.tensor_copy(dn[:, COLS:2 * COLS], bank[7][:, :]).then_inc(S.dn_dve, 1)

            dve.memset(zeros[:, :], 0.0)
            dve.memset(v_ext[:, :, :, DK:DK + 1], 1.0)
            dve.memset(zT[:, :, 0:2], 0.0)
            for i in range(2):
                dve.memset(cums[i][:, 0:P], 0.0)
                last = dve.memset(maxs[i][:, 0:P], 0.0)
            last.then_inc(dve_consts, 1)
            dve.wait_ge(dve_consts, 1)
            dve.wait_ge(consts, 1)

            for l in range(DEPTH):
                if l == 0:
                    dve.wait_ge(cols_ready, 1)
                    for i in range(DEPTH):
                        dve.tensor_copy(b_ada_col[:, i, :], bank[7][:, 64 * i:64 * i + NMOD])
                        last = dve.tensor_copy(w_conv_col[:, i, :], bank[7][:, 128 + 16 * i:128 + 16 * i + 3 * CH])
                    last.then_inc(cols_copied, 1)
                    dve.wait_ge(cols_copied, 1)
                dve.wait_ge(ada_ext, 12 * l + 4)
                dve.tensor_tensor(mod[:, 0, :], bank[6][:, 0:KC], b_ada_col[:, l, 0:KC], ALU.add)
                last = dve.scalar_tensor_tensor(out=mod[:, 1, :], in0=bank[6][:, KC:2 * KC], scalar=1.0,
                                                in1=b_ada_col[:, l, KC:2 * KC], op0=ALU.add, op1=ALU.add)
                last.then_inc(mod_ready, 1)
                dve.wait_ge(mod_ready, 2 * l + 1)
                modulate(l, 0)
                dve.wait_ge(gates_ready, l + 1)
                dve.wait_ge(small_landed[l], 16 * 2)
                link(dve.tensor_scalar(gate_pre, bank[3][0:8, 0:SEQ], b_gates_col[:, l:l + 1], None, ALU.add))
                dve.scalar_tensor_tensor(out=gate_neg, in0=gate_pre, scalar=-1.0, in1=gate_pre,
                                         op0=ALU.mult, op1=ALU.min).then_inc(neg_ready, 1)
                dve.wait_ge(ln_ready, l + 1)
                link(dve.scalar_tensor_tensor(out=cums[0][:, P:P + SEQ], in0=gate_pre, scalar=0.0,
                                              in1=gate_ln, op0=ALU.min, op1=ALU.subtract))
                for i in range(8):
                    s, a, b = 1 << i, cums[i % 2], cums[1 - i % 2]
                    ins = dve.tensor_tensor(b[:, P:P + SEQ], a[:, P:P + SEQ], a[:, P - s:P - s + SEQ], ALU.add)
                    if i < 7:
                        link(ins)
                ins.then_inc(cum_ready, 1)
                dve.wait_ge(aF_ready, l + 1)
                dve.tensor_copy(a_row, bank[2][0:HEADS, 0:SEQ])
                link(dve.tensor_copy(maxs[0][:, P:P + SEQ], bank[2][0:HEADS, 0:SEQ]))
                for i in range(8):
                    s, a, b = 1 << i, maxs[i % 2], maxs[1 - i % 2]
                    link(dve.tensor_tensor(b[:, P:P + SEQ], a[:, P:P + SEQ], a[:, P - s:P - s + SEQ], ALU.max))
                link(dve.tensor_scalar(maxs[0][:, P:P + SEQ], maxs[0][:, P:P + SEQ], 0.0, None, ALU.max))
                dve.tensor_scalar(neg_g, maxs[0][:, P:P + SEQ], -1.0, None, ALU.mult)
                dve.scalar_tensor_tensor(out=neg_m, in0=bank[2][0:HEADS, SEQ:2 * SEQ], scalar=-1.0,
                                         in1=maxs[0][:, P:P + SEQ], op0=ALU.mult, op1=ALU.subtract).then_inc(rows_ready, 1)
                dve.wait_ge(bcast_ready, l + 1)
                link(dve.tensor_copy(a_col[:, :, :], bank[3][:, 0:16].rearrange("p (t c) -> p t c", t=T)[:, :, 0:4]))
                for h in range(HEADS):
                    g = bank[h // 2][:, (h % 2) * SEQ:(h % 2 + 1) * SEQ]
                    dve.scalar_tensor_tensor(out=expo[:, h, 0:SEQ], in0=g, scalar=a_col[:, 0, h:h + 1],
                                             in1=causal[:, 0:SEQ], op0=ALU.add, op1=ALU.add)
                    dve.scalar_tensor_tensor(out=expo[:, h, SEQ:SEQ + P], in0=g[:, P:SEQ], scalar=a_col[:, 1, h:h + 1],
                                             in1=causal[:, SEQ:SEQ + P], op0=ALU.add, op1=ALU.add).then_inc(arg_ready, 1)
                for h in range(HEADS):
                    dve.wait_ge(score_done, HEADS * l + h + 1)
                    dve.wait_ge(exp_ready, HEADS * l + h + 1)
                    dve.scalar_tensor_tensor(out=expo[:, h, :], in0=bank[h][:, 0:SEQ + P], scalar=SCALE,
                                             in1=expo[:, h, :], op0=ALU.mult, op1=ALU.mult).then_inc(prob_ready, 1)
                dve.wait_ge(proj_act, 16 * l + 12)
                link(dve.tensor_scalar(o_sig[:, :, :], o_sig[:, :, :], 1.0, None, ALU.add))
                link(dve.reciprocal(o_sig[:, :, :], o_sig[:, :, :]))
                dve.wait_ge(expm_ready, l + 1)
                for h in range(HEADS):
                    dve.wait_ge(pv_done, HEADS * l + h + 1)
                    last = dve.tensor_copy(den[:, :, h:h + 1], bank[h][:, 0:2 * DK + 2].rearrange("p (t d) -> p t d", t=T)[:, :, DK:DK + 1])
                link(last)
                link(dve.scalar_tensor_tensor(out=dmax[:, :, :], in0=den[:, :, :], scalar=-1.0, in1=den[:, :, :],
                                              op0=ALU.mult, op1=ALU.max))
                link(dve.tensor_tensor(dmax[:, :, :], dmax[:, :, :], exp_neg_m[:, :, :], ALU.max))
                link(dve.reciprocal(dmax[:, :, :], dmax[:, :, :]))
                for h in range(HEADS):
                    for t in range(T):
                        last = dve.tensor_scalar(hb[:, t, h * DK:(h + 1) * DK], bank[h][:, t * (DK + 1):t * (DK + 1) + DK],
                                                 dmax[:, t, h:h + 1], None, ALU.mult)
                link(last)
                for t in range(T):
                    for h in range(HEADS):
                        last = dve.bn_stats(stats_h[:, t * HEADS + h, :], hb[:, t, h * DK:(h + 1) * DK])
                link(last)
                for i in range(T * HEADS):
                    last = dve.bn_aggr(mv_h[:, i, :], stats_h[:, i, :])
                link(last)
                dve.tensor_scalar(var[:, :], mv_h[:, :, 1], EPS, None, ALU.add).then_inc(hvar_ready, 1)
                for q in range(CH):
                    dve.wait_ge(proj_done, NBLK * l + 17 + q)
                    dve.wait_ge(proj_act, 16 * l + 13 + q)
                    dve.tensor_tensor(zT[:, q, 2:2 + SEQ], ccT[:, q, :], bank[4 + q][:, 0:SEQ], ALU.mult).then_inc(proj_dve, 1)
                newton(0, T * HEADS, hrs_ready, l + 1)
                for t in range(T):
                    for h in range(HEADS):
                        i = t * HEADS + h
                        last = dve.tensor_scalar(hb[:, t, h * DK:(h + 1) * DK], hb[:, t, h * DK:(h + 1) * DK],
                                                 mv_h[:, i, 0:1], rstd[:, i:i + 1], ALU.subtract, ALU.mult)
                link(last)
                dve.wait_ge(rows_landed, 16 * 7 * l + 16 * 7)
                link(dve.tensor_tensor(hb[:, :, :], hb[:, :, :], mh_w[:, :].unsqueeze(1).to_broadcast([P, T, WM]), ALU.mult))
                dve.tensor_tensor(hb[:, :, :], hb[:, :, :], o_sig[:, :, :], ALU.mult).then_inc(h_ready, 1)
                for q in range(CH):
                    tap = lambda k: w_conv_col[:, l, k * CH + q:k * CH + q + 1]
                    dve.wait_ge(proj_dve, 8 * l + q + 1)
                    link(dve.tensor_scalar(convT[:, :], zT[:, q, 0:SEQ], tap(0), None, ALU.mult))
                    for k in (1, 2):
                        link(dve.scalar_tensor_tensor(out=convT[:, :], in0=zT[:, q, k:k + SEQ], scalar=tap(k),
                                                      in1=convT[:, :], op0=ALU.mult, op1=ALU.add))
                    dve.wait_ge(proj_done, NBLK * l + 21 + q)
                    dve.tensor_tensor(mixT[:, CH + q, :], convT[:, :], bank[4 + q][:, 0:SEQ], ALU.mult).then_inc(proj_dve, 1)
                    dve.wait_ge(proj_dve, 8 * l + CH + q + 1)
                gate_rows(l, 0, GATE1)
                dve.wait_ge(gate_row_ready, 4 * l + 2)
                residual_norm(l, 0, between=lambda: shift_scale(l))
                modulate(l, 1)

                dve.wait_ge(logT_done, l + 1)
                dve.wait_ge(route_landed, 16 * 4 * DEPTH)
                dve.tensor_scalar(logT[:, :], bank[6][0:G + EXPERTS, 0:SEQ], b_route_col[:, l:l + 1], None,
                                  ALU.add).then_inc(logT_copied, 1)
                dve.wait_ge(logit_done, l + 1)
                link(dve.tensor_copy(logit[:, :, :], bank[6][:, 0:64].rearrange("p (t c) -> p t c", t=T)[:, :, 0:G + EXPERTS]))
                gl = logit[:, :, 0:G]
                el = logit[:, :, G:G + EXPERTS].rearrange("p t (g e) -> p t g e", g=G)
                link(dve.tensor_reduce(gmax[:, :, :], gl, AX.X, ALU.max))
                dve.tensor_tensor(dif[:, :, 0:G], gl, gmax[:, :, :].to_broadcast([P, T, G]), ALU.subtract)
                first_of(gl, gmax[:, :, :], grp1[:, :, :])
                link(dve.tensor_tensor(ew[:, :, :, :], el, grp1[:, :, :].unsqueeze(3).to_broadcast([P, T, G, E]), ALU.mult))
                link(dve.tensor_reduce(sel[:, :, :], ew[:, :, :, :].rearrange("p t g e -> p t e g"), AX.X, ALU.add))
                link(dve.tensor_reduce(m1[:, :, :], sel[:, :, :], AX.X, ALU.max))
                first_of(sel[:, :, :], m1[:, :, :], top1[:, :, :])
                link(dve.scalar_tensor_tensor(out=sel2[:, :, :], in0=top1[:, :, :], scalar=MASKED, in1=sel[:, :, :],
                                              op0=ALU.mult, op1=ALU.add))
                link(dve.tensor_reduce(m2[:, :, :], sel2[:, :, :], AX.X, ALU.max))
                dve.tensor_tensor(dif[:, :, G:G + 1], m2[:, :, :], m1[:, :, :], ALU.subtract).then_inc(dif_ready, 1)
                first_of(sel2[:, :, :], m2[:, :, :], top2[:, :, :])
                link(dve.tensor_tensor(both[:, :, :], top1[:, :, :], top2[:, :, :], ALU.add))
                dve.tensor_tensor(mask[:, :, :].rearrange("p t (g e) -> p t g e", g=G),
                                  both[:, :, :].unsqueeze(2).to_broadcast([P, T, G, E]),
                                  grp1[:, :, :].unsqueeze(3).to_broadcast([P, T, G, E]), ALU.mult).then_inc(mask_ready, 1)
                dve.wait_ge(pos_done, l + 1)
                link(dve.scalar_tensor_tensor(out=pos[:, :, :], in0=bank[6][:, 0:2 * EXPERTS].rearrange("p (t e) -> p t e", t=T),
                                              scalar=1.0, in1=mask[:, :, :], op0=ALU.add, op1=ALU.mult))
                link(dve.tensor_scalar(pos[:, :, :], pos[:, :, :], -1.0, None, ALU.add))
                dve.tensor_reduce(pmax[:, :], pos[:, :, :].rearrange("p t e -> p (t e)"), AX.X, ALU.max).then_inc(pmax_ready, 1)
                build_disp(main, 0, 0)
                gate_rows(l, 1, GATE2)
                dve.wait_ge(dexp_ready, l + 1)
                dve.tensor_reduce(wsum[:, :, 0:1], dexp[:, :, 0:G], AX.X, ALU.add)
                link(dve.tensor_scalar(wsum[:, :, 1:2], dexp[:, :, G:G + 1], 1.0, None, ALU.add))
                link(dve.tensor_tensor(wsum[:, :, 0:1], wsum[:, :, 0:1], wsum[:, :, 1:2], ALU.mult))
                link(dve.reciprocal(wsum[:, :, 0:1], wsum[:, :, 0:1]))
                link(dve.tensor_tensor(wboth[:, :, :], top2[:, :, :], dexp[:, :, G:G + 1].to_broadcast([P, T, E]), ALU.mult))
                link(dve.tensor_tensor(wboth[:, :, :], wboth[:, :, :], top1[:, :, :], ALU.add))
                link(dve.tensor_tensor(wboth[:, :, :], wboth[:, :, :], wsum[:, :, 0:1].to_broadcast([P, T, E]), ALU.mult))
                link(dve.tensor_tensor(comb[:, :, :].rearrange("p t (g e) -> p t g e", g=G),
                                       wboth[:, :, :].unsqueeze(2).to_broadcast([P, T, G, E]),
                                       grp1[:, :, :].unsqueeze(3).to_broadcast([P, T, G, E]), ALU.mult))
                build_dispw(main, 0, 0)

                xg_half(main, PAIRS * l)
                dve.wait_ge(pmaxT_done, l + 1)
                link(dve.tensor_reduce(pall[:, :], bank[5][0:1, 0:P], AX.X, ALU.max))
                dve.tensor_scalar(flag[:, l:l + 1], pall[:, :], float(CAP), None, ALU.is_ge).then_inc(flag_ready, 1)
                build(main, 2, 1)

                def pair(p, b, more=True, final=False):
                    n = PAIRS * l + p
                    hidden(main, n)
                    if not final:
                        xg_half(main, n + 1)
                    combine_copy(main, n)
                    if more:
                        build(main, 2 * p + 4, b)
                    down_copy(main, n)

                pair(0, 0)
                with dve.Fori(0, (PAIRS - 4) // 2) as i:
                    pair(2 * i + 1, 1)
                    pair(2 * i + 2, 0)
                pair(PAIRS - 3, 1)
                pair(PAIRS - 2, 0, more=False)
                pair(PAIRS - 1, 1, more=False, final=True)
                more = dve.value_load(flag[0:1, l:l + 1])
                with dve.If(more != 0):
                    S = over[l]
                    with dve.Fori(0, ROUNDS - 1) as r:
                        dve.wait_ge(S.disp, r * PAIRS)
                        dve.tensor_scalar(pos[:, :, :], pos[:, :, :], -float(CAP), None, ALU.add).then_inc(S.added, 1)
                        dve.wait_ge(S.added, (r + 1) * (PAIRS + 1) - PAIRS)
                        dve.memset(scm[:, :, :], 0.0)
                        with dve.Fori(0, PAIRS) as p:
                            n = r * PAIRS + p
                            dve.wait_ge(S.cT, n)
                            build(S, 2 * p, 0)
                            xg_half(S, n)
                            hidden(S, n)
                            combine_copy(S, n)
                            down_copy(S, n)
                        dve.wait_ge(S.added, (r + 1) * (PAIRS + 1))
                residual_norm(l, 1)


_INS = ['x', 'c', 'w_ada', 'b_ada', 'w_in', 'b_gates', 'mh_norm_w', 'w_conv', 'w_out', 'ln1_g', 'ln1_b',
        'w_grp', 'b_grp', 'w_router', 'b_router', 'w_gate', 'w_up', 'w_down', 'ln2_g', 'ln2_b']


def kernel(**inputs):
    import numpy as _np
    import concourse.bacc as _bacc
    from concourse import mybir as _mybir
    from concourse.bass_utils import run_bass_kernel_spmd as _run

    nc = _bacc.Bacc("TRN2", target_bir_lowering=False, num_devices=1)
    arrays, args = {}, []
    for name in _INS:
        a = _np.ascontiguousarray(inputs[name])
        arrays[f"in_{name}_dram"] = a
        args.append(nc.dram_tensor(f"in_{name}_dram", a.shape, _mybir.dt.from_np(a.dtype), kind="ExternalInput").ap())
    args.append(nc.dram_tensor("out_dram", arrays["in_x_dram"].shape, _mybir.dt.float32, kind="ExternalOutput").ap())
    trunk_kernel(nc, *args)
    r = _run(nc, [arrays], core_ids=[0])
    return r.results[0]["out_dram"]
```
